# Optimizing a Trainium2 kernel written in Bass

```python
import math
import jax, jax.numpy as jnp
from jax import lax
import numpy as np

D_MODEL = 2048
BATCH = 1
SEQ = 256
DEPTH = 1

ATTN_WIDTH = D_MODEL // 2
CONV_WIDTH = D_MODEL - ATTN_WIDTH
D_MIX = ATTN_WIDTH + CONV_WIDTH
DIFF_HEAD_DIM = 64
N_DIFF_HEADS = ATTN_WIDTH // (2 * DIFF_HEAD_DIM)
CONV_KERNEL = 31
Q_BLOCK = 128
PEER_HEADS = 8
PEER_KEYS = 128
N_EXPERTS = PEER_KEYS * PEER_KEYS
PEER_TOPK = 16
PEER_KEY_DIM = 256
PEER_TOK_BLOCK = 64
EPS = 1e-6
IN_COLS = 3 * ATTN_WIDTH + 2 * CONV_WIDTH

kernel_name = "hybrid_diffattn_conformer_peer_block"

def rms_norm(x, g):
    xf = x.astype(jnp.float32)
    y = xf * lax.rsqrt(jnp.mean(xf * xf, axis=-1, keepdims=True) + EPS)
    return (y * g.astype(jnp.float32)).astype(x.dtype)

def layer_norm(x, g, b):
    xf = x.astype(jnp.float32)
    mu = jnp.mean(xf, axis=-1, keepdims=True)
    var = jnp.mean(jnp.square(xf - mu), axis=-1, keepdims=True)
    y = (xf - mu) * lax.rsqrt(var + EPS)
    return (y * g.astype(jnp.float32) + b.astype(jnp.float32)).astype(x.dtype)

def lambda_init_fn(layer_idx):
    return 0.8 - 0.6 * math.exp(-0.3 * layer_idx)

def alibi_slopes(n_heads):
    return 2.0 ** (-8.0 * (np.arange(n_heads, dtype=np.float32) + 1.0) / n_heads)

def diff_attention(qkv, lq1, lk1, lq2, lk2, g_subln, lambda_init):
    B, S, _ = qkv.shape
    H, Dh = N_DIFF_HEADS, DIFF_HEAD_DIM
    q, k, v = jnp.split(qkv, 3, axis=-1)
    q = q.reshape(B, S, H, 2, Dh).transpose(0, 2, 3, 1, 4)
    k = k.reshape(B, S, H, 2, Dh).transpose(0, 2, 3, 1, 4)
    v = v.reshape(B, S, H, 2 * Dh).transpose(0, 2, 1, 3)
    lam = (jnp.exp(jnp.sum(lq1.astype(jnp.float32) * lk1.astype(jnp.float32)))
           - jnp.exp(jnp.sum(lq2.astype(jnp.float32) * lk2.astype(jnp.float32)))
           + lambda_init)
    slopes = jnp.asarray(alibi_slopes(H))
    scale = 1.0 / math.sqrt(Dh)
    n_blocks = S // Q_BLOCK
    q_blocks = jnp.moveaxis(q.reshape(B, H, 2, n_blocks, Q_BLOCK, Dh), 3, 0)
    starts = jnp.arange(n_blocks, dtype=jnp.int32) * Q_BLOCK
    k_pos = jnp.arange(S, dtype=jnp.int32)

    def block_fn(args):
        qb, start = args
        q_pos = start + jnp.arange(Q_BLOCK, dtype=jnp.int32)
        s = jnp.einsum('bhmqd,bhmkd->bhmqk', qb, k).astype(jnp.float32) * scale
        dist = (q_pos[:, None] - k_pos[None, :])
        bias = -slopes[:, None, None, None] * dist.astype(jnp.float32)
        s = jnp.where(dist >= 0, s + bias, -jnp.inf)
        p = jax.nn.softmax(s, axis=-1)
        a = p[:, :, 0] - lam * p[:, :, 1]
        return jnp.einsum('bhqk,bhkd->bhqd', a.astype(v.dtype), v)

    o = lax.map(block_fn, (q_blocks, starts))
    o = o.transpose(1, 0, 3, 2, 4).reshape(B, S, H, 2 * Dh)
    o = rms_norm(o, g_subln) * (1.0 - lambda_init)
    return o.reshape(B, S, ATTN_WIDTH)

def conformer_conv(glu_in, conv_w, conv_b, ln_g, ln_b):
    a, gate = jnp.split(glu_in, 2, axis=-1)
    u = a * jax.nn.sigmoid(gate)
    y = lax.conv_general_dilated(
        u, conv_w[:, None, :].astype(u.dtype), window_strides=(1,),
        padding=[(CONV_KERNEL - 1, 0)],
        dimension_numbers=('NWC', 'WIO', 'NWC'),
        feature_group_count=CONV_WIDTH)
    y = y + conv_b
    y = layer_norm(y, ln_g, ln_b)
    return jax.nn.silu(y)

def peer_ffn(h, w_q, k1, k2, u_tab, v_tab):
    B, S, D = h.shape
    T = B * S
    half = PEER_KEY_DIM // 2
    q = (h @ w_q).reshape(T, PEER_HEADS, PEER_KEY_DIM)
    hf = h.reshape(T, D)
    nb = T // PEER_TOK_BLOCK
    q_b = q.reshape(nb, PEER_TOK_BLOCK, PEER_HEADS, PEER_KEY_DIM)
    h_b = hf.reshape(nb, PEER_TOK_BLOCK, D)

    def block_fn(args):
        hb, qb = args
        s1 = jnp.einsum('thd,kd->thk', qb[..., :half], k1)
        s2 = jnp.einsum('thd,kd->thk', qb[..., half:], k2)
        v1, i1 = lax.top_k(s1, PEER_TOPK)
        v2, i2 = lax.top_k(s2, PEER_TOPK)
        cand = (v1[..., :, None] + v2[..., None, :]).reshape(
            PEER_TOK_BLOCK, PEER_HEADS, PEER_TOPK * PEER_TOPK)
        cand_idx = (i1[..., :, None] * PEER_KEYS + i2[..., None, :]).reshape(
            PEER_TOK_BLOCK, PEER_HEADS, PEER_TOPK * PEER_TOPK)
        top, pos = lax.top_k(cand, PEER_TOPK)
        idx = jnp.take_along_axis(cand_idx, pos, axis=-1)
        g = jax.nn.softmax(top.astype(jnp.float32), axis=-1)
        u = u_tab[idx]
        vv = v_tab[idx]
        act = jax.nn.gelu(jnp.einsum('thkd,td->thk', u, hb).astype(jnp.float32),
                          approximate=False) * g
        return jnp.einsum('thk,thkd->td', act.astype(vv.dtype), vv)

    out = lax.map(block_fn, (h_b, q_b))
    return out.reshape(B, S, D)

def setup_inputs(seed: int = 0) -> dict:
    key = jax.random.key(seed)
    ks = jax.random.split(key, 24)
    D = D_MODEL
    f32 = jnp.float32
    nrm = lambda k, shape, s: jax.random.normal(k, shape, f32) * s
    gain = lambda k, shape: 1.0 + nrm(k, shape, 0.05)
    return {
        "x": nrm(ks[0], (BATCH, SEQ, D), 1.0),
        "c": nrm(ks[1], (BATCH, D), 1.0),
        "w_ada": nrm(ks[2], (DEPTH, D, 6 * D), 0.2 * D ** -0.5),
        "b_ada": nrm(ks[3], (DEPTH, 6 * D), 0.01),
        "g_pre_mix": gain(ks[4], (DEPTH, D)),
        "g_post_mix": gain(ks[5], (DEPTH, D)),
        "g_pre_ffn": gain(ks[6], (DEPTH, D)),
        "g_post_ffn": gain(ks[7], (DEPTH, D)),
        "w_in": nrm(ks[8], (DEPTH, D, IN_COLS), D ** -0.5),
        "lambda_q1": nrm(ks[9], (DEPTH, DIFF_HEAD_DIM), 0.1),
        "lambda_k1": nrm(ks[10], (DEPTH, DIFF_HEAD_DIM), 0.1),
        "lambda_q2": nrm(ks[11], (DEPTH, DIFF_HEAD_DIM), 0.1),
        "lambda_k2": nrm(ks[12], (DEPTH, DIFF_HEAD_DIM), 0.1),
        "g_subln": gain(ks[13], (DEPTH, 2 * DIFF_HEAD_DIM)),
        "conv_w": nrm(ks[14], (DEPTH, CONV_KERNEL, CONV_WIDTH), CONV_KERNEL ** -0.5),
        "conv_b": nrm(ks[15], (DEPTH, CONV_WIDTH), 0.01),
        "conv_ln_g": gain(ks[16], (DEPTH, CONV_WIDTH)),
        "conv_ln_b": nrm(ks[17], (DEPTH, CONV_WIDTH), 0.01),
        "w_out": nrm(ks[18], (DEPTH, D_MIX, D), D_MIX ** -0.5),
        "peer_wq": nrm(ks[19], (DEPTH, D, PEER_HEADS * PEER_KEY_DIM), D ** -0.5),
        "peer_k1": nrm(ks[20], (DEPTH, PEER_KEYS, PEER_KEY_DIM // 2), (PEER_KEY_DIM // 2) ** -0.5),
        "peer_k2": nrm(ks[21], (DEPTH, PEER_KEYS, PEER_KEY_DIM // 2), (PEER_KEY_DIM // 2) ** -0.5),
        "peer_u": nrm(ks[22], (DEPTH, N_EXPERTS, D), D ** -0.5),
        "peer_v": nrm(ks[23], (DEPTH, N_EXPERTS, D), (PEER_HEADS * PEER_TOPK) ** -0.5),
    }

def reference(x, c, w_ada, b_ada, g_pre_mix, g_post_mix, g_pre_ffn, g_post_ffn,
              w_in, lambda_q1, lambda_k1, lambda_q2, lambda_k2, g_subln,
              conv_w, conv_b, conv_ln_g, conv_ln_b, w_out,
              peer_wq, peer_k1, peer_k2, peer_u, peer_v):
    for l in range(DEPTH):
        lambda_init = lambda_init_fn(l)
        mod = jax.nn.silu(c) @ w_ada[l] + b_ada[l]
        sh_m, sc_m, gt_m, sh_f, sc_f, gt_f = [m[:, None, :] for m in jnp.split(mod, 6, axis=-1)]

        h = rms_norm(x, g_pre_mix[l]) * (1.0 + sc_m) + sh_m
        proj = h @ w_in[l]
        qkv = proj[..., :3 * ATTN_WIDTH]
        glu_in = proj[..., 3 * ATTN_WIDTH:]
        y_attn = diff_attention(qkv, lambda_q1[l], lambda_k1[l], lambda_q2[l], lambda_k2[l],
                                g_subln[l], lambda_init)
        y_conv = conformer_conv(glu_in, conv_w[l], conv_b[l], conv_ln_g[l], conv_ln_b[l])
        mix = jnp.concatenate([y_attn, y_conv], axis=-1) @ w_out[l]
        x = x + gt_m * rms_norm(mix, g_post_mix[l])

        h = rms_norm(x, g_pre_ffn[l]) * (1.0 + sc_f) + sh_f
        ff = peer_ffn(h, peer_wq[l], peer_k1[l], peer_k2[l], peer_u[l], peer_v[l])
        x = x + gt_f * rms_norm(ff, g_post_ffn[l])
    return x


_drawn_inputs = setup_inputs


def setup_inputs(seed=0):
    import zlib

    import numpy as np

    out = dict(_drawn_inputs(seed))
    spreads = {}
    factors = {'g_pre_mix': 3.672,
     'g_post_mix': 4.355,
     'g_post_ffn': 8.0,
     'lambda_q1': 8.0,
     'lambda_k1': 8.0,
     'lambda_k2': 31.777,
     'g_subln': 5.113,
     'conv_b': 8.0,
     'conv_ln_g': 5.733,
     'conv_ln_b': 8.0,
     'lambda_q2': 2.778}
    for name, (base, spread) in spreads.items():
        noise = np.random.default_rng([zlib.crc32(name.encode()), seed]).standard_normal(out[name].shape)
        drawn = base * np.exp(spread * noise) if base else spread * noise
        out[name] = __import__('jax').numpy.asarray(drawn.astype(out[name].dtype))
    for name, factor in factors.items():
        out[name] = (out[name] * factor).astype(out[name].dtype)
    return out
```

```python
from contextlib import ExitStack
import math

import concourse.bass as bass
from concourse import mybir

P = 128
D = 2048
T = 256
KC = D // P
HEADS = 8
HEAD_DIM = 64
TAPS = 31
PAD = TAPS - 1
CONV_CHUNKS = 8
POOL_CONV_CHUNKS = 3
PEER_HEADS = 8
KEYS = 128
TOPK = 16
EPS = 1e-6
LAMBDA_INIT = 0.8 - 0.6 * math.exp(-0.3 * 0)
SCALE = 1.0 / math.sqrt(HEAD_DIM)
SLOPES = [2.0 ** (-8.0 * (h + 1.0) / HEADS) for h in range(HEADS)]
FAR = 1e30
LOWEST = -3e38

RAW = 4
UNIT = 1024
UCH = UNIT // P
IN_BLOCKS = 40
BLOCKS = D // P
EXPERT_BLOCKS = KEYS

U_ADA = 0
U_IN = U_ADA + 2 * 2 * KC
IN_MIXED = KC
U_IN_PLAIN = U_IN + 8 * IN_MIXED
IN_PLAIN = IN_BLOCKS // 2 - IN_MIXED
U_OUT = U_IN_PLAIN + 4 * IN_PLAIN
U_WQ = U_OUT + 4 * BLOCKS
U_UP = U_WQ + 4 * BLOCKS
U_DOWN = U_UP + 2 * EXPERT_BLOCKS
S_IN = 0
S_OUT = S_IN + 2 * IN_BLOCKS
S_WQ = S_OUT + 2 * BLOCKS
S_UP = S_WQ + 2 * BLOCKS
S_DOWN = S_UP + 2 * EXPERT_BLOCKS
B_IN = 0
B_OUT = B_IN + IN_BLOCKS
B_WQ = B_OUT + BLOCKS
B_UP = B_WQ + BLOCKS
B_END = B_UP + EXPERT_BLOCKS

F32 = mybir.dt.float32
F32R = mybir.dt.float32r
U32 = mybir.dt.uint32
ALU = mybir.AluOpType
ACT = mybir.ActivationFunctionType
AXX = mybir.AxisListType.X


def at(i, step, first):
    return first if i is None else i * step + first


def build_block(nc, x, c, w_ada, b_ada, g_vecs, w_in, lambdas, g_subln, conv_w, conv_vecs,
                w_out, peer_wq, peer_keys, peer_u, peer_v, out):
    with ExitStack() as ctx:
        def sb(name, shape, dt=F32):
            return ctx.enter_context(nc.sbuf_tensor(name, shape, dt))

        def sem(name):
            return ctx.enter_context(nc.semaphore(name))

        big = sb("big", [P, KEYS * T])
        routed_v = big[:, :].rearrange("p (i t) -> p i t", t=T)
        routed_by_token = big[:, :].rearrange("p (i t) -> p t i", t=T)

        def region(start, *shape):
            n = int(math.prod(shape))
            v = big[:, start:start + n]
            if len(shape) == 2:
                v = v.rearrange("p (a b) -> p a b", b=shape[1])
            if len(shape) == 3:
                v = v.rearrange("p (a b c) -> p a b c", b=shape[1], c=shape[2])
            return v

        xT = region(0, KC, T)
        hT = region(4096, KC, T)
        proj = region(8192, IN_BLOCKS, T)
        convT = region(8192, CONV_CHUNKS, T)
        conv_sq = region(10240, CONV_CHUNKS, T)
        mixT = region(8192, KC, T)
        squares = region(12288, KC, T)
        acc = region(18432, 2, D)
        upad = region(22528, CONV_CHUNKS, T + PAD)
        oT = region(24832, HEADS, T)
        v_tok = region(26880, 2 * HEADS, P)
        probs = region(28928, 2, 2, 384)
        aT = region(30464, 2, 384)
        distm = region(31232, 384)
        conv_wt = region(31616, CONV_CHUNKS, TAPS)
        conv_v = region(31864, 3, CONV_CHUNKS)
        lam_in = region(31888, 4, HEAD_DIM)
        stat = region(32144, 2, T)
        o_sq = region(4096, HEADS * T)
        o_rs = region(6144, HEADS * T)
        s_all = region(12288, 16, 2 * KEYS)
        rt = 22528
        st = region(rt, 2, KEYS)
        st2 = region(rt + 256, 2, KEYS)
        cand = region(rt + 512, TOPK, TOPK)
        cand2 = region(rt + 768, TOPK * TOPK)
        pick_a = region(rt + 1024, TOPK, TOPK)
        pick_b = region(rt + 1280, TOPK, TOPK)
        v16 = region(rt + 1536, 2, TOPK)
        top16 = region(rt + 1568, TOPK)
        ix16f = region(rt + 1584, 2, TOPK)
        pos_f = region(rt + 1616, 2, TOPK)
        gates = region(rt + 1664, 16, TOPK)
        gate_sum = region(rt + 1920, 16)
        idx1 = region(rt + 2048, 16, TOPK)
        idx2 = region(rt + 2304, 16, TOPK)
        ix16 = sb("ix16", [P, 2, TOPK], U32)
        pos16 = sb("pos16", [P, 3, TOPK], U32)

        a_hi = sb("a_hi", [P, KC, T], F32R)
        a_lo = sb("a_lo", [P, KC, T], F32R)
        raw = sb("raw", [P, RAW, UNIT])
        w_hi = sb("w_hi", [P, 2, UNIT], F32R)
        w_lo = sb("w_lo", [P, 2, UNIT], F32R)

        ones = sb("ones", [P, P])
        ident = sb("ident", [P, P])
        iota = sb("iota", [P, P])
        cT = sb("cT", [P, KC])
        mod_b = sb("mod_b", [P, 6 * KC])
        mod = sb("mod", [P, 6, KC])
        gv = sb("gv", [P, 4, KC])
        gsub = sb("gsub", [P, 1])
        keysT = sb("keysT", [P, 2, KEYS])
        rs = sb("rs", [P, T])
        sel_T = sb("sel_T", [P, 3, T])
        oh1 = sb("oh1", [P, 2, 2, P])
        oh2 = sb("oh2", [P, 2, 2, P])
        gel = sb("gel", [P, 2, T])
        pool_tmp = gel[:, 0, :]
        first_col = sb("first_col", [P, 2, 2])
        nothing = sb("nothing", [P, 2])
        tiny = sb("tiny", [P, 32])
        lam_sum, lam_exp, neg_lam = tiny[:, 0:2], tiny[:, 2:4], tiny[:, 4:5]
        mx = [tiny[:, 8:12], tiny[:, 12:16]]
        sums = [tiny[:, 16:20], tiny[:, 20:24]]
        rcp = [tiny[:, 24:28], tiny[:, 28:32]]

        ps = ctx.enter_context(nc.psum_tensor("ps", [P, 8, 512], F32))
        x_saved = nc.dram_tensor("x_saved", (P, KC * T), F32, kind="Internal").ap()

        landed = [sem(f"landed{j}") for j in range(RAW)]
        x_in, small_in = sem("x_in"), sem("small_in")
        consumed, hi_ready, split_used = sem("consumed"), sem("hi_ready"), sem("split_used")
        gemm_evac = sem("gemm_evac")
        consts, pool, first_cols = sem("consts"), sem("pool"), sem("first_cols")
        vec, act_d = sem("vec"), sem("act_d")
        sq_ready, ss_ready, var_ready, rs_ready = (sem("sq_ready"), sem("ss_ready"), sem("var_ready"),
                                                   sem("rs_ready"))
        silu_c, xr_ready, mod_sum, mod_ready = sem("silu_c"), sem("xr_ready"), sem("mod_sum"), sem("mod_ready")
        h_hi, h_ready = sem("h_hi"), sem("h_ready")
        gate_sig, glu_ready, pool_conv = sem("gate_sig"), sem("glu_ready"), sem("pool_conv")
        s_ready, s_read, neg_max, exp_done = sem("s_ready"), sem("s_read"), sem("neg_max"), sem("exp_done")
        a_ready, aT_ready, aT_copied = sem("a_ready"), sem("aT_ready"), sem("aT_copied")
        o_ready, o_copied, vt_ready, vt_copied = sem("o_ready"), sem("o_copied"), sem("vt_ready"), sem("vt_copied")
        lam_dots, lam_e = sem("lam_dots"), sem("lam_e")
        conv_ready, conv_stat = sem("conv_ready"), sem("conv_stat")
        conv_sq_ready, z_ready, y_ready = sem("conv_sq_ready"), sem("z_ready"), sem("y_ready")
        o_sq_ready, o_ss, o_var, o_rs_ready = sem("o_sq_ready"), sem("o_ss"), sem("o_var"), sem("o_rs_ready")
        conv_var, conv_rs, conv_n = sem("conv_var"), sem("conv_rs"), sem("conv_n")
        x2_ready, x2_saved, x2_back = sem("x2_ready"), sem("x2_saved"), sem("x2_back")
        sc_ready, sc_copied = sem("sc_ready"), sem("sc_copied")
        gate_in, gate_exp, sel_ready, selT_ready, selT_copied = (sem("gate_in"), sem("gate_exp"),
                                                                 sem("sel_ready"), sem("selT_ready"),
                                                                 sem("selT_copied"))
        oh1_ready, oh2_ready, oh_used = sem("oh1_ready"), sem("oh2_ready"), sem("oh_used")
        w_evac, routed = sem("w_evac"), sem("routed")
        at_hi, at_lo, ff_done, ff_copied, out_ready, out_done = (sem("at_hi"), sem("at_lo"), sem("ff_done"),
                                                                 sem("ff_copied"), sem("out_ready"),
                                                                 sem("out_done"))

        ada = w_ada.rearrange("(k p) n -> k p n", p=P)
        N_SMALL = 9
        block = ctx.enter_context(nc.Block())

        @block.sync
        def _(sp):
            def bring(u0, i, per, src, first=False):
                if not first:
                    sp.wait_ge(consumed, at(i, per, u0 - RAW + 1))
                sp.dma_start(raw[:, u0 % RAW, :], src).then_inc(landed[u0 % RAW], 16)

            def ada_unit(group, kc, half):
                col = group * D + half * UNIT
                if isinstance(kc, int):
                    return ada[kc, :, col:col + UNIT]
                return ada[bass.ds(kc, 1), :, col:col + UNIT].rearrange("o p n -> (o p) n")

            def unit_of(w, b, half):
                if isinstance(b, int):
                    return w[b, :, half * UNIT:(half + 1) * UNIT]
                return w[bass.ds(b, 1), :, half * UNIT:(half + 1) * UNIT].rearrange("o p n -> (o p) n")

            for j in range(4):
                bring(U_ADA + j, None, 4, ada_unit(j // 2, 0, j % 2), first=True)
            with sp.Fori(1, KC) as i:
                for j in range(4):
                    bring(U_ADA + j, i, 4, ada_unit(j // 2, i, j % 2))
            with sp.Fori(0, IN_MIXED) as i:
                for j in range(8):
                    src = (ada_unit(2 + j // 4, i, j % 2) if j % 4 >= 2 else unit_of(w_in, i * 2 + j // 4, j % 2))
                    bring(U_IN + j, i, 8, src)
            with sp.Fori(0, IN_PLAIN) as i:
                for j in range(4):
                    bring(U_IN_PLAIN + j, i, 4, unit_of(w_in, i * 2 + (2 * IN_MIXED + j // 2), j % 2))
            for base, w, group in ((U_OUT, w_out, 4), (U_WQ, peer_wq, 5)):
                with sp.Fori(0, BLOCKS // 2) as i:
                    for j in range(8):
                        src = (ada_unit(group, i * 2 + j // 4, j % 2) if j % 4 >= 2
                               else unit_of(w, i * 2 + j // 4, j % 2))
                        bring(base + j, i, 8, src)
            for base, w in ((U_UP, peer_u), (U_DOWN, peer_v)):
                with sp.Fori(0, EXPERT_BLOCKS // 2) as i:
                    for j in range(4):
                        bring(base + j, i, 4, unit_of(w, i * 2 + j // 2, j % 2))
            sp.wait_ge(ff_done, 1)
            sp.dma_start(xT.rearrange("p a b -> p (a b)"), x_saved).then_inc(x2_back, 16)
            for q in range(4):
                sp.wait_ge(out_ready, q + 1)
                sp.dma_start(out[:, q * 1024:(q + 1) * 1024],
                             mixT[:, 4 * q:4 * q + 4, :].rearrange("p a b -> p (a b)")).then_inc(out_done, 16)
            sp.wait_ge(out_done, 64)

        @block.gpsimd
        def _(gp):
            gp.memset(ones[:, :], 1.0).then_inc(consts, 1)
            gp.memset(ident[:, :], 0.0).then_inc(pool, 1)
            gp.wait_ge(pool, 1)
            gp.affine_select(out=ident[:, :], in_=ident[:, :], compare_op=ALU.not_equal, fill=1.0, base=0,
                             pattern=[[-1, P]], channel_multiplier=1).then_inc(consts, 1)
            gp.iota(iota[:, :], pattern=[[1, P]], base=0, channel_multiplier=0,
                    allow_small_or_imprecise_dtypes=True).then_inc(consts, 1)
            gp.iota(distm[:, 0:128], pattern=[[-1, 128]], base=0, channel_multiplier=1,
                    allow_small_or_imprecise_dtypes=True).then_inc(pool, 1)
            gp.iota(distm[:, 128:384], pattern=[[-1, 256]], base=128, channel_multiplier=1,
                    allow_small_or_imprecise_dtypes=True).then_inc(pool, 1)
            gp.wait_ge(pool, 3)
            gp.affine_select(out=distm[:, 0:128], in_=distm[:, 0:128], compare_op=ALU.is_ge, fill=FAR, base=0,
                             pattern=[[-1, 128]], channel_multiplier=1).then_inc(consts, 1)
            gp.affine_select(out=distm[:, 128:384], in_=distm[:, 128:384], compare_op=ALU.is_ge, fill=FAR,
                             base=128, pattern=[[-1, 256]], channel_multiplier=1).then_inc(consts, 1)
            gp.memset(upad[:, :, 0:PAD], 0.0).then_inc(pool, 1)
            gp.wait_ge(pool, 4)
            gp.wait_ge(gate_sig, 1)
            gp.tensor_tensor(upad[:, :, PAD:PAD + T], proj[:, 0:8, :], proj[:, 8:16, :], ALU.mult)\
                .then_inc(glu_ready, 1)
            gp.wait_ge(glu_ready, 1)
            gp.wait_ge(small_in, 16 * N_SMALL)
            n = 4
            for ch in range(CONV_CHUNKS - POOL_CONV_CHUNKS, CONV_CHUNKS):
                gp.tensor_scalar(convT[:, ch, :], upad[:, ch, 0:T], conv_wt[:, ch, 0:1], conv_v[:, 0, ch:ch + 1],
                                 ALU.mult, ALU.add).then_inc(pool, 1)
                n += 1
                for j in range(1, TAPS):
                    gp.wait_ge(pool, n)
                    gp.tensor_scalar(pool_tmp, upad[:, ch, j:j + T], conv_wt[:, ch, j:j + 1], None, ALU.mult)\
                        .then_inc(pool, 1)
                    n += 1
                    gp.wait_ge(pool, n)
                    done = gp.tensor_tensor(convT[:, ch, :], convT[:, ch, :], pool_tmp, ALU.add)
                    done.then_inc(pool, 1)
                    n += 1
            gp.wait_ge(pool, n)
            gp.engine_nop().then_inc(pool_conv, 1) if False else gp.memset(pool_tmp, 0.0).then_inc(pool_conv, 1)

            def first_key(i, j):
                gp.tensor_copy(first_col[:, j % 2, :], sel_T[:, 0, bass.ds(at(i, 8, 2 * j), 2)])\
                    .then_inc(first_cols, 1)
                gp.wait_ge(first_cols, at(i, 4, j + 1))
                gp.tensor_tensor(nothing[:, 1:2], nothing[:, 0:1], nothing[:, 0:1], ALU.add)
                for t in range(2):
                    done = gp.tensor_scalar(oh1[:, j % 2, t, :], iota[:, :], first_col[:, j % 2, t:t + 1], None,
                                            ALU.is_equal)
                done.then_inc(oh1_ready, 1)

            gp.wait_ge(selT_copied, 1)
            gp.memset(nothing[:, 0:1], 0.0).then_inc(pool, 1)
            gp.wait_ge(pool, n + 1)
            for j in range(4):
                if j >= 2:
                    gp.wait_ge(oh_used, j - 1)
                first_key(None, j)
            with gp.Fori(1, T // 8) as i:
                for j in range(4):
                    gp.wait_ge(oh_used, at(i, 4, j - 1))
                    first_key(i, j)

        @block.scalar
        def _(act):
            act.dma_start(xT.rearrange("p a b -> p (a b)"), x).then_inc(x_in, 16)
            act.dma_start(cT[:, :], c).then_inc(small_in, 16)
            act.dma_start(mod_b[:, :], b_ada).then_inc(small_in, 16)
            act.dma_start(gv[:, :, :], g_vecs).then_inc(small_in, 16)
            act.dma_start(gsub[:, :], g_subln).then_inc(small_in, 16)
            act.dma_start(conv_wt, conv_w).then_inc(small_in, 16)
            act.dma_start(conv_v, conv_vecs).then_inc(small_in, 16)
            act.dma_start(lam_in, lambdas.partition_broadcast(P)).then_inc(small_in, 16)
            act.dma_start(keysT[:, 0, :], peer_keys[0]).then_inc(small_in, 16)
            act.dma_start(keysT[:, 1, :], peer_keys[1]).then_inc(small_in, 16)
            act.wait_ge(x_in, 16)
            act.activation(squares, xT, ACT.Square).then_inc(sq_ready, 1)
            act.wait_ge(small_in, 16 * N_SMALL)
            act.activation(cT[:, :], cT[:, :], ACT.Silu).then_inc(silu_c, 1)
            act.wait_ge(lam_dots, 2)
            act.activation(lam_exp, lam_sum, ACT.Exp).then_inc(lam_e, 1)
            act.wait_ge(var_ready, 1)
            act.activation(rs[:, :], rs[:, :], ACT.Sqrt).then_inc(rs_ready, 1)

            def modulated(shift, n):
                act.wait_ge(mod_ready, n)
                for kc in range(KC):
                    act.activation(a_hi[:, kc, :], hT[:, kc, :], ACT.Identity, bias=mod[:, shift, kc:kc + 1],
                                   scale=mod[:, shift + 1, kc:kc + 1]).then_inc(h_hi, 1)

            act.wait_ge(xr_ready, 1)
            modulated(0, 1)

            def hi(u0, s0, i, uper, sper, first=False):
                act.wait_ge(landed[u0 % RAW], at(i, uper // RAW * 16, (u0 // RAW + 1) * 16))
                if not first:
                    act.wait_ge(split_used, at(i, sper, s0 - 1))
                act.activation(w_hi[:, s0 % 2, :], raw[:, u0 % RAW, :], ACT.Copy).then_inc(hi_ready, 1)

            def evac(dst, b0, i, per):
                act.wait_ge(split_used, at(i, 2 * per, 2 * b0 + 2))
                act.activation(dst, ps[:, b0 % 2, 0:T], ACT.Copy).then_inc(gemm_evac, 1)

            def chunk(buf, b0, i, per):
                if i is None:
                    return buf[:, b0, :]
                return buf[:, bass.ds(i * per + b0, 1), :].rearrange("p o t -> p (o t)")

            for j in range(4):
                hi(U_IN + (j if j < 2 else j + 2), S_IN + j, None, 8, 4, first=j < 2)
                if j == 3:
                    evac(chunk(proj, 0, None, 2), B_IN, None, 2)
            with act.Fori(1, IN_MIXED) as i:
                for j in range(4):
                    hi(U_IN + (j if j < 2 else j + 2), S_IN + j, i, 8, 4)
                    if j % 2:
                        evac(chunk(proj, j // 2 - 1, i, 2), B_IN + j // 2 - 1 + (0 if j == 3 else 0), i, 2)
            b0 = 2 * IN_MIXED
            for j in range(4):
                hi(U_IN_PLAIN + j, S_IN + 2 * b0 + j, None, 4, 4)
                if j % 2:
                    evac(chunk(proj, b0 + j // 2 - 1, None, 2), B_IN + b0 + j // 2 - 1, None, 2)
            act.wait_ge(gemm_evac, 16)
            act.activation(proj[:, 8:16, :], proj[:, 8:16, :], ACT.Sigmoid).then_inc(gate_sig, 1)
            with act.Fori(1, IN_PLAIN) as i:
                for j in range(4):
                    hi(U_IN_PLAIN + j, S_IN + 2 * b0 + j, i, 4, 4)
                    if j % 2:
                        evac(chunk(proj, b0 + j // 2 - 1, i, 2), B_IN + b0 + j // 2 - 1, i, 2)
            evac(chunk(proj, IN_BLOCKS - 1, None, 2), B_IN + IN_BLOCKS - 1, None, 2)

            def exps(h):
                act.wait_ge(neg_max, h + 1)
                for m in range(2):
                    for qb, (a, b) in enumerate(((0, 128), (128, 384))):
                        done = act.activation(probs[:, h % 2, m, a:b], probs[:, h % 2, m, a:b], ACT.Exp,
                                              bias=mx[h % 2][:, 2 * m + qb:2 * m + qb + 1], scale=SCALE,
                                              accum_out=sums[h % 2][:, 2 * m + qb:2 * m + qb + 1])
                done.then_inc(exp_done, 1)

            exps(0)
            exps(1)
            for h in range(HEADS):
                act.wait_ge(aT_ready, h + 1)
                if h >= 2:
                    act.wait_ge(o_ready, h - 1)
                act.activation(aT[:, h % 2, :], ps[:, 0, 0:384], ACT.Copy).then_inc(aT_copied, 1)
                act.wait_ge(o_ready, h + 1)
                act.activation(oT[:, h, :], ps[:, 1, 0:T], ACT.Copy).then_inc(o_copied, 1)
                if h + 2 < HEADS:
                    exps(h + 2)
            act.wait_ge(o_copied, HEADS)
            act.activation(o_sq, oT.rearrange("p a b -> p (a b)"), ACT.Square).then_inc(o_sq_ready, 1)
            act.wait_ge(o_var, 1)
            act.activation(o_rs, o_rs, ACT.Sqrt).then_inc(o_rs_ready, 1)
            act.wait_ge(conv_stat, 1)
            act.activation(conv_sq, convT, ACT.Square).then_inc(conv_sq_ready, 1)
            act.wait_ge(conv_var, 1)
            act.activation(stat[:, 1, :], stat[:, 1, :], ACT.Sqrt).then_inc(conv_rs, 1)
            act.wait_ge(y_ready, 1)
            act.activation(a_hi[:, 0:8, :], oT, ACT.Copy).then_inc(h_hi, 1)
            act.wait_ge(conv_n, 1)
            for ch in range(CONV_CHUNKS):
                act.activation(convT[:, ch, :], convT[:, ch, :], ACT.Silu, bias=conv_v[:, 2, ch:ch + 1],
                               scale=conv_v[:, 1, ch:ch + 1]).then_inc(z_ready, 1)
            act.wait_ge(z_ready, CONV_CHUNKS)
            act.activation(a_hi[:, 8:16, :], convT, ACT.Copy).then_inc(h_hi, 1)

            def mix_out(b0, i, per):
                evac(chunk(mixT, b0, i, per), B_OUT + b0, i, per)
                act.wait_ge(gemm_evac, at(i, per, B_OUT + b0 + 1))
                act.activation(chunk(squares, b0, i, per), chunk(mixT, b0, i, per), ACT.Square)\
                    .then_inc(sq_ready, 1)

            def with_ada(ubase, sbase, put):
                for j in range(4):
                    hi(ubase + (j if j < 2 else j + 2), sbase + j, None, 8, 4)
                    if j == 3:
                        put(0, None, 2)
                with act.Fori(1, BLOCKS // 2) as i:
                    for j in range(4):
                        hi(ubase + (j if j < 2 else j + 2), sbase + j, i, 8, 4)
                        if j % 2:
                            put(j // 2 - 1, i, 2)
                put(BLOCKS - 1, None, 2)

            act.wait_ge(h_ready, KC + 2)
            with_ada(U_OUT, S_OUT, mix_out)
            act.wait_ge(var_ready, 2)
            act.activation(rs[:, :], rs[:, :], ACT.Sqrt).then_inc(rs_ready, 1)
            act.wait_ge(x2_ready, 1)
            act.dma_start(x_saved, xT.rearrange("p a b -> p (a b)")).then_inc(x2_saved, 16)
            act.activation(squares, xT, ACT.Square).then_inc(sq_ready, 1)
            act.wait_ge(var_ready, 3)
            act.activation(rs[:, :], rs[:, :], ACT.Sqrt).then_inc(rs_ready, 1)
            act.wait_ge(xr_ready, 2)
            modulated(3, 3)

            with_ada(U_WQ, S_WQ, lambda b0, i, per: evac(chunk(mixT, b0, i, per), B_WQ + b0, i, per))
            for n in range(8):
                act.wait_ge(sc_ready, n + 1)
                act.activation(s_all[:, 2 * n:2 * n + 2, :], ps[:, 2 + n % 2, :].rearrange("p (a b) -> p a b", a=2),
                               ACT.Copy).then_inc(sc_copied, 1)
            act.wait_ge(gate_in, 1)
            act.activation(gates, gates, ACT.Exp).then_inc(gate_exp, 1)

            def weights_out(i, j):
                act.wait_ge(oh_used, at(i, 4, 2 * j + 2))
                act.activation(routed_by_token[:, bass.ds(at(i, 8, 4 * j), 4), :],
                               ps[:, 2 + j, :].rearrange("p (a b) -> p a b", a=4), ACT.Copy).then_inc(w_evac, 1)

            act.wait_ge(x2_saved, 16)
            with act.Fori(0, T // 8) as i:
                for j in range(2):
                    weights_out(i, j)

            def gelu(b0, i, per, early=False):
                act.wait_ge(split_used, at(i, 2 * per, 2 * (B_UP + b0) + 2))
                if not early:
                    act.wait_ge(routed, at(i, per, b0 - 1))
                act.activation(gel[:, b0 % 2, :], ps[:, (B_UP + b0) % 2, 0:T], ACT.Gelu).then_inc(gemm_evac, 1)

            for j in range(4):
                hi(U_UP + j, S_UP + j, None, 4, 4)
                if j == 3:
                    gelu(0, None, 2, early=True)
            for j in range(4):
                hi(U_UP + 4 + j, S_UP + 4 + j, None, 4, 4)
                if j % 2:
                    gelu(1 + j // 2, None, 2, early=j == 1)
            with act.Fori(2, EXPERT_BLOCKS // 2) as i:
                for j in range(4):
                    hi(U_UP + j, S_UP + j, i, 4, 4)
                    if j % 2:
                        gelu(j // 2 - 1, i, 2)
            gelu(EXPERT_BLOCKS - 1, None, 2)

            def down(i):
                for j in range(4):
                    if j % 2 == 0:
                        act.wait_ge(split_used, at(i, 4, S_DOWN + j - 2))
                        act.activation(a_hi[:, j // 2, :], chunk(routed_v, j // 2, i, 2), ACT.Copy)\
                            .then_inc(at_hi, 1)
                    hi(U_DOWN + j, S_DOWN + j, i, 4, 4)

            act.wait_ge(split_used, 2 * B_END)
            act.wait_ge(routed, EXPERT_BLOCKS)
            down(None)
            with act.Fori(1, EXPERT_BLOCKS // 2) as i:
                down(i)
            for n in range(8):
                act.wait_ge(ff_copied, n + 1)
                act.activation(squares[:, 2 * n:2 * n + 2, :], mixT[:, 2 * n:2 * n + 2, :], ACT.Square)\
                    .then_inc(sq_ready, 1)
            act.wait_ge(var_ready, 4)
            act.activation(rs[:, :], rs[:, :], ACT.Sqrt).then_inc(rs_ready, 1)

        @block.tensor
        def _(pe):
            def sum_squares(n_sq, src, each=1):
                for kc in range(KC):
                    pe.wait_ge(sq_ready, n_sq[kc])
                    done = pe.matmul(ps[:, 7, 0:T], ones[:, :], src[:, kc, :], start=kc == 0, stop=kc == KC - 1)
                done.then_inc(ss_ready, 1)

            def modulation(groups, u_last, bank):
                pe.wait_ge(consumed, u_last)
                for g, a in groups:
                    for dc in range(KC):
                        done = pe.matmul(ps[:, bank, g * KC + dc:g * KC + dc + 1], acc[:, a, dc * P:(dc + 1) * P],
                                         ones[:, 0:1], start=True, stop=True)
                done.then_inc(mod_sum, 1)

            def product(bank, u0, s0, b0, i, uper, per, free=True, act_base=None):
                if free:
                    pe.wait_ge(gemm_evac, at(i, per, b0 - 1))
                for half in range(2):
                    pe.wait_ge(consumed, at(i, uper, u0 + half + 1))
                    for k in range(UCH):
                        kc = half * UCH + k
                        if act_base is not None:
                            pe.wait_ge(h_ready, act_base[kc])
                        for n, (w, a) in enumerate(((w_hi, a_hi), (w_hi, a_lo), (w_lo, a_hi))):
                            done = pe.matmul(ps[:, bank, 0:T], w[:, half, k * P:(k + 1) * P], a[:, kc, :],
                                             start=kc == 0 and n == 0, stop=kc == KC - 1 and n == 2)
                    done.then_inc(split_used, 1)

            pe.wait_ge(consts, 5)
            sum_squares([1] * KC, squares)
            modulation(((0, 0), (1, 1)), U_IN, 6)
            first = [kc + 1 for kc in range(KC)]
            for j in range(2):
                product(j % 2, U_IN + 4 * j, S_IN + 2 * j, B_IN + j, None, 8, 2, free=False,
                        act_base=first if j == 0 else None)
            with pe.Fori(1, IN_MIXED) as i:
                for j in range(2):
                    product(j, U_IN + 4 * j, S_IN + 2 * j, B_IN + j, i, 8, 2)
            with pe.Fori(0, IN_PLAIN) as i:
                for j in range(2):
                    product(j, U_IN_PLAIN + 2 * j, 0, B_IN + 2 * IN_MIXED + j, i, 4, 2)

            pe.wait_ge(gemm_evac, IN_BLOCKS)
            modulation(((2, 0), (3, 1)), U_IN_PLAIN, 6)

            def scores(h):
                if h >= 2:
                    pe.wait_ge(s_read, h - 1)
                q, k = proj[:, 16 + h, :], proj[:, 24 + h, :]
                for m in range(2):
                    r = slice(64 * m, 64 * m + 64)
                    bank = 2 + 2 * (h % 2) + m
                    pe.matmul(ps[:, bank, 0:128], q[r, 0:128], k[r, 0:128], start=True, stop=True)
                    done = pe.matmul(ps[:, bank, 128:384], q[r, 128:256], k[r, :], start=True, stop=True)
                done.then_inc(s_ready, 1)

            scores(0)
            scores(1)
            for n in range(4):
                if n >= 2:
                    pe.wait_ge(vt_copied, n - 1)
                if n == 0:
                    pe.wait_ge(mod_ready, 2)
                for j in range(4):
                    done = pe.transpose(ps[:, 6 + n % 2, j * P:(j + 1) * P],
                                        proj[:, 32 + 2 * n + j // 2, (j % 2) * P:(j % 2 + 1) * P], ident[:, :])
                done.then_inc(vt_ready, 1)
            for h in range(HEADS):
                pe.wait_ge(a_ready, h + 1)
                if h >= 1:
                    pe.wait_ge(aT_copied, h)
                for j in range(3):
                    done = pe.transpose(ps[:, 0, j * P:(j + 1) * P], probs[:, h % 2, 0, j * P:(j + 1) * P],
                                        ident[:, :])
                done.then_inc(aT_ready, 1)
                if h + 2 < HEADS:
                    scores(h + 2)
                pe.wait_ge(aT_copied, h + 1)
                if h == 0:
                    pe.wait_ge(vt_copied, 4)
                if h >= 1:
                    pe.wait_ge(o_copied, h)
                pe.matmul(ps[:, 1, 0:128], v_tok[:, 2 * h, :], aT[:, h % 2, 0:128], start=True, stop=True)
                pe.matmul(ps[:, 1, 128:256], v_tok[:, 2 * h, :], aT[:, h % 2, 128:256], start=True, stop=False)
                pe.matmul(ps[:, 1, 128:256], v_tok[:, 2 * h + 1, :], aT[:, h % 2, 256:384], start=False,
                          stop=True).then_inc(o_ready, 1)
            pe.wait_ge(o_sq_ready, 1)
            for n in range(4):
                done = pe.matmul(ps[:, 2 + n, :], ones[:, :], o_sq[:, n * 512:(n + 1) * 512], start=True, stop=True)
            done.then_inc(o_ss, 1)
            pe.wait_ge(pool_conv, 1)
            pe.wait_ge(conv_ready, 1)
            for ch in range(CONV_CHUNKS):
                done = pe.matmul(ps[:, 7, 0:T], ones[:, :], convT[:, ch, :], start=ch == 0,
                                 stop=ch == CONV_CHUNKS - 1)
            done.then_inc(ss_ready, 1)
            pe.wait_ge(conv_sq_ready, 1)
            for ch in range(CONV_CHUNKS):
                done = pe.matmul(ps[:, 6, 0:T], ones[:, :], conv_sq[:, ch, :], start=ch == 0,
                                 stop=ch == CONV_CHUNKS - 1)
            done.then_inc(ss_ready, 1)

            mix_base = [KC + 1] * 8 + [KC + 2] * 8
            for base, b_base, act_base in ((U_OUT, B_OUT, mix_base), (U_WQ, B_WQ, [KC + 3 + kc for kc in range(KC)])):
                for j in range(2):
                    product(j, base + 4 * j, 0, b_base + j, None, 8, 2, act_base=act_base if j == 0 else None)
                with pe.Fori(1, BLOCKS // 2) as i:
                    for j in range(2):
                        product(j, base + 4 * j, 0, b_base + j, i, 8, 2)
                if base == U_OUT:
                    modulation(((4, 0),), U_WQ, 6)
                    sum_squares([kc + 2 for kc in range(KC)], squares)
                    sum_squares([KC + 2] * KC, squares)
                else:
                    pe.wait_ge(gemm_evac, B_UP)
                    modulation(((5, 1),), U_UP, 6)
            for n in range(8):
                if n >= 2:
                    pe.wait_ge(sc_copied, n - 1)
                for j in range(4):
                    r, half = 2 * n + j // 2, j % 2
                    tt, h = r // 8, r % 8
                    done = pe.matmul(ps[:, 2 + n % 2, j * KEYS:(j + 1) * KEYS],
                                     mixT[:, 2 * h + half, tt * P:(tt + 1) * P], keysT[:, half, :],
                                     start=True, stop=True)
                done.then_inc(sc_ready, 1)
            pe.wait_ge(sc_copied, 8)
            pe.wait_ge(sel_ready, 1)
            for n, src in enumerate((idx1, idx2, gates)):
                flat = src.rearrange("p r k -> p (r k)")
                for tt in range(2):
                    done = pe.transpose(ps[:, 2 + n // 2, (n % 2) * T + tt * P:(n % 2) * T + (tt + 1) * P],
                                        flat[:, tt * P:(tt + 1) * P], ident[:, :])
            done.then_inc(selT_ready, 1)

            def weights(i, j, early):
                for s in range(2):
                    n = 2 * j + s
                    pe.wait_ge(oh1_ready, at(i, 4, n + 1))
                    pe.wait_ge(oh2_ready, at(i, 4, n + 1))
                    if s == 0 and not early:
                        pe.wait_ge(w_evac, at(i, 2, j - 1))
                    for t in range(2):
                        done = pe.matmul(ps[:, 2 + j, (2 * s + t) * P:(2 * s + t + 1) * P], oh2[:, s, t, :],
                                         oh1[:, s, t, :], start=True, stop=True)
                    done.then_inc(oh_used, 1)

            pe.wait_ge(selT_copied, 1)
            for j in range(2):
                weights(None, j, True)
            with pe.Fori(1, T // 8) as i:
                for j in range(2):
                    weights(i, j, False)

            with pe.Fori(0, EXPERT_BLOCKS // 2) as i:
                for j in range(2):
                    product(j, U_UP + 2 * j, 0, B_UP + j, i, 4, 2)

            def down(i):
                for j in range(4):
                    blk = j // 2
                    if j % 2 == 0:
                        pe.wait_ge(at_lo, at(i, 2, blk + 1))
                    pe.wait_ge(consumed, at(i, 4, U_DOWN + j + 1))
                    for k in range(UCH):
                        dt = (j % 2) * UCH + k
                        for n, (w, a) in enumerate(((w_hi, a_hi), (w_hi, a_lo), (w_lo, a_hi))):
                            done = pe.matmul(ps[:, dt // 2, (dt % 2) * T:(dt % 2 + 1) * T],
                                             w[:, j % 2, k * P:(k + 1) * P], a[:, blk, :],
                                             start=i is None and blk == 0 and n == 0 and dt % 2 == 0,
                                             stop=False, skip_group_check=True)
                    done.then_inc(split_used, 1)
                return done

            pe.wait_ge(gemm_evac, B_END)
            down(None)
            with pe.Fori(1, EXPERT_BLOCKS // 2) as i:
                down(i)
            pe.wait_ge(split_used, S_DOWN + 2 * EXPERT_BLOCKS)
            pe.drain().then_inc(ff_done, 1)
            pe.wait_ge(ff_copied, 8)
            sum_squares([2 * KC - KC + 3 + kc // 2 for kc in range(KC)], squares)

        @block.vector
        def _(dve):
            count = [0]

            def link(ins):
                count[0] += 1
                ins.then_inc(vec, 1)
                dve.wait_ge(vec, count[0])

            def bcast_t(v, n=KC):
                return v[:, None, :].to_broadcast([P, n, T])

            def variance(bank, n, eps_of, dst, done):
                link(dve.tensor_scalar(dst, bank, 1.0 / n, EPS, ALU.mult, ALU.add))
                dve.reciprocal(dst, dst).then_inc(done, 1)

            link(dve.memset(acc, 0.0))
            dve.wait_ge(small_in, 16 * N_SMALL)
            for n in range(2):
                link(dve.tensor_tensor(lam_in[:, 2 * n, :], lam_in[:, 2 * n, :], lam_in[:, 2 * n + 1, :], ALU.mult))
                dve.tensor_reduce(lam_sum[:, n:n + 1], lam_in[:, 2 * n, :], AXX, ALU.add).then_inc(lam_dots, 1)
            link(dve.tensor_scalar(gsub[:, :], gsub[:, :], 1.0 - LAMBDA_INIT, None, ALU.mult))
            dve.wait_ge(ss_ready, 1)
            variance(ps[:, 7, 0:T], D, EPS, rs[:, :], var_ready)
            dve.wait_ge(rs_ready, 1)
            dve.tensor_tensor(hT, xT, bcast_t(rs), ALU.mult).then_inc(xr_ready, 1)
            dve.wait_ge(lam_e, 1)
            link(dve.tensor_tensor(neg_lam, lam_exp[:, 1:2], lam_exp[:, 0:1], ALU.subtract))
            link(dve.tensor_scalar(neg_lam, neg_lam, -LAMBDA_INIT, None, ALU.add))

            def ada_step(u0, i, per, a, half, kc, back):
                dve.wait_ge(landed[u0 % RAW], at(i, per // RAW * 16, (u0 // RAW + 1) * 16))
                if back is not None:
                    dve.wait_ge(consumed, at(i, per, u0 + 1 - back))
                dst = acc[:, a, half * UNIT:(half + 1) * UNIT]
                col = cT[:, kc:kc + 1] if isinstance(kc, int) else cT[:, bass.ds(kc, 1)]
                dve.scalar_tensor_tensor(dst, raw[:, u0 % RAW, :], col, dst, ALU.mult, ALU.add)\
                    .then_inc(consumed, 1)

            def lo(u0, s0, i, uper, sper, first=False):
                dve.wait_ge(hi_ready, at(i, sper, s0 + 1))
                dve.tensor_tensor(w_lo[:, s0 % 2, :], raw[:, u0 % RAW, :], w_hi[:, s0 % 2, :].bitcast(F32),
                                  ALU.subtract).then_inc(consumed, 1)

            dve.wait_ge(silu_c, 1)
            for j in range(4):
                ada_step(U_ADA + j, None, 4, j // 2, j % 2, 0, None)
            with dve.Fori(1, KC) as i:
                for j in range(4):
                    ada_step(U_ADA + j, i, 4, j // 2, j % 2, i, 4)

            def mod_add(groups, n, bank=6):
                dve.wait_ge(mod_sum, n)
                a, b = groups[0], groups[-1] + 1
                link(dve.tensor_tensor(mod[:, a:b, :], ps[:, bank, a * KC:b * KC].rearrange("p (a b) -> p a b", b=KC),
                                       mod_b[:, a * KC:b * KC].rearrange("p (a b) -> p a b", b=KC), ALU.add))

            mod_add((0, 1), 1)
            dve.scalar_tensor_tensor(mod[:, 1, :], mod[:, 1, :], 1.0, gv[:, 0, :], ALU.add, ALU.mult)\
                .then_inc(mod_ready, 1)
            link(dve.memset(acc, 0.0))

            def modulated(shift, n_hi):
                dve.wait_ge(mod_ready, 1 if shift == 0 else 3)
                for kc in range(KC):
                    dve.wait_ge(h_hi, n_hi + kc + 1)
                    link(dve.tensor_scalar(hT[:, kc, :], hT[:, kc, :], mod[:, shift + 1, kc:kc + 1],
                                           mod[:, shift, kc:kc + 1], ALU.mult, ALU.add))
                    dve.tensor_tensor(a_lo[:, kc, :], hT[:, kc, :], a_hi[:, kc, :].bitcast(F32), ALU.subtract)\
                        .then_inc(h_ready, 1)

            modulated(0, 0)

            def mixed_step(ubase, sbase, i, put, first=False):
                for j in range(8):
                    if j % 4 < 2:
                        s = 2 * (j // 4) + j % 2
                        lo(ubase + j, sbase + s, i, 8, 4)
                    else:
                        put(j, i)

            def in_ada(j, i):
                ada_step(U_IN + j, i, 8, j // 4, j % 2, 0 if i is None else i, 8)

            mixed_step(U_IN, S_IN, None, in_ada)
            with dve.Fori(1, IN_MIXED) as i:
                mixed_step(U_IN, S_IN, i, in_ada)
            with dve.Fori(0, IN_PLAIN) as i:
                for j in range(4):
                    lo(U_IN_PLAIN + j, S_IN + 4 * IN_MIXED + j, i, 4, 4)

            mod_add((2, 3), 2)
            dve.tensor_tensor(mod[:, 2, :], mod[:, 2, :], gv[:, 1, :], ALU.mult).then_inc(mod_ready, 1)
            link(dve.memset(acc, 0.0))

            def head_scores(h):
                dve.wait_ge(s_ready, h + 1)
                if h >= 2:
                    dve.wait_ge(aT_ready, h - 1)
                for m in range(2):
                    done = dve.scalar_tensor_tensor(probs[:, h % 2, m, :], distm, -SLOPES[h] / SCALE,
                                                    ps[:, 2 + 2 * (h % 2) + m, 0:384], ALU.mult, ALU.add)
                    if m == 0:
                        link(done)
                done.then_inc(s_read, 1)
                dve.wait_ge(s_read, h + 1)
                for m in range(2):
                    for qb, (a, b) in enumerate(((0, 128), (128, 384))):
                        done = dve.tensor_reduce(mx[h % 2][:, 2 * m + qb:2 * m + qb + 1], probs[:, h % 2, m, a:b],
                                                 AXX, ALU.max)
                link(done)
                dve.tensor_scalar(mx[h % 2], mx[h % 2], -SCALE, None, ALU.mult).then_inc(neg_max, 1)

            def head_combine(h):
                p, r = probs[:, h % 2], rcp[h % 2]
                dve.wait_ge(exp_done, h + 1)
                link(dve.reciprocal(r, sums[h % 2]))
                link(dve.tensor_scalar(r[:, 2:4], r[:, 2:4], neg_lam, None, ALU.mult))
                for qb, (a, b) in enumerate(((0, 128), (128, 384))):
                    done = dve.tensor_scalar(p[:, 1, a:b], p[:, 1, a:b], r[:, 2 + qb:3 + qb], None, ALU.mult)
                link(done)
                for qb, (a, b) in enumerate(((0, 128), (128, 384))):
                    done = dve.scalar_tensor_tensor(p[:, 0, a:b], p[:, 0, a:b], r[:, qb:qb + 1], p[:, 1, a:b],
                                                    ALU.mult, ALU.add)
                done.then_inc(a_ready, 1)

            def conv(ch):
                link(dve.tensor_scalar(convT[:, ch, :], upad[:, ch, 0:T], conv_wt[:, ch, 0:1],
                                       conv_v[:, 0, ch:ch + 1], ALU.mult, ALU.add))
                for j in range(1, TAPS):
                    done = dve.scalar_tensor_tensor(convT[:, ch, :], upad[:, ch, j:j + T], conv_wt[:, ch, j:j + 1],
                                                    convT[:, ch, :], ALU.mult, ALU.add)
                    link(done)

            head_scores(0)
            head_scores(1)
            for n in range(4):
                dve.wait_ge(vt_ready, n + 1)
                dve.tensor_copy(v_tok[:, 4 * n:4 * n + 4, :], ps[:, 6 + n % 2, :].rearrange("p (a b) -> p a b", a=4))\
                    .then_inc(vt_copied, 1)
            dve.wait_ge(glu_ready, 1)
            for h in range(HEADS):
                head_combine(h)
                if h + 2 < HEADS:
                    head_scores(h + 2)
                if h < CONV_CHUNKS - POOL_CONV_CHUNKS:
                    conv(h)
            dve.memset(tiny[:, 5:6], 0.0).then_inc(conv_ready, 1)
            dve.wait_ge(o_ss, 1)
            for n in range(4):
                done = dve.tensor_scalar(o_rs[:, n * 512:(n + 1) * 512], ps[:, 2 + n, :], 1.0 / P, EPS, ALU.mult,
                                         ALU.add)
            link(done)
            dve.reciprocal(o_rs, o_rs).then_inc(o_var, 1)
            dve.wait_ge(ss_ready, 2)
            link(dve.tensor_scalar(stat[:, 0, :], ps[:, 7, 0:T], 1.0 / (P * CONV_CHUNKS), None, ALU.mult))
            dve.tensor_tensor(convT, convT, bcast_t(stat[:, 0, :], 8), ALU.subtract).then_inc(conv_stat, 1)
            dve.wait_ge(o_rs_ready, 1)
            flat_o = oT.rearrange("p a b -> p (a b)")
            dve.scalar_tensor_tensor(flat_o, flat_o, gsub[:, 0:1], o_rs, ALU.mult, ALU.mult).then_inc(y_ready, 1)
            dve.wait_ge(ss_ready, 3)
            variance(ps[:, 6, 0:T], P * CONV_CHUNKS, EPS, stat[:, 1, :], conv_var)
            dve.wait_ge(h_hi, KC + 1)
            dve.wait_ge(y_ready, 1)
            dve.tensor_tensor(a_lo[:, 0:8, :], oT, a_hi[:, 0:8, :].bitcast(F32), ALU.subtract).then_inc(h_ready, 1)
            dve.wait_ge(conv_rs, 1)
            dve.tensor_tensor(convT, convT, bcast_t(stat[:, 1, :], 8), ALU.mult).then_inc(conv_n, 1)
            dve.wait_ge(h_hi, KC + 2)
            dve.tensor_tensor(a_lo[:, 8:16, :], convT, a_hi[:, 8:16, :].bitcast(F32), ALU.subtract)\
                .then_inc(h_ready, 1)

            def group_ada(ubase, a):
                def put(j, i):
                    kc = j // 4 if i is None else i * 2 + j // 4
                    ada_step(ubase + j, i, 8, a, j % 2, kc, 4)
                return put

            def group_loop(ubase, sbase, a):
                mixed_step(ubase, sbase, None, group_ada(ubase, a))
                with dve.Fori(1, BLOCKS // 2) as i:
                    mixed_step(ubase, sbase, i, group_ada(ubase, a))

            group_loop(U_OUT, S_OUT, 0)

            mod_add((4,), 3)
            dve.scalar_tensor_tensor(mod[:, 4, :], mod[:, 4, :], 1.0, gv[:, 2, :], ALU.add, ALU.mult)\
                .then_inc(mod_ready, 1)
            dve.wait_ge(ss_ready, 4)
            variance(ps[:, 7, 0:T], D, EPS, rs[:, :], var_ready)
            dve.wait_ge(rs_ready, 2)
            for kc in range(KC):
                done = dve.scalar_tensor_tensor(mixT[:, kc, :], mixT[:, kc, :], mod[:, 2, kc:kc + 1], rs[:, :],
                                                ALU.mult, ALU.mult)
            link(done)
            dve.tensor_tensor(xT, xT, mixT, ALU.add).then_inc(x2_ready, 1)
            dve.wait_ge(ss_ready, 5)
            variance(ps[:, 7, 0:T], D, EPS, rs[:, :], var_ready)
            dve.wait_ge(rs_ready, 3)
            dve.tensor_tensor(hT, xT, bcast_t(rs), ALU.mult).then_inc(xr_ready, 1)
            modulated(3, KC + 2)

            group_loop(U_WQ, S_WQ, 1)
            mod_add((5,), 4)
            link(dve.tensor_tensor(mod[:, 5, :], mod[:, 5, :], gv[:, 3, :], ALU.mult))

            dve.wait_ge(sc_copied, 8)
            base = count[0]
            with dve.Fori(0, 2 * PEER_HEADS) as r:
                step = [0]

                def chain(ins, before_max=False):
                    step[0] += 1
                    ins.then_inc(vec, 1)
                    dve.wait_ge(vec, r * CH + (base + step[0]))
                    if before_max:
                        dve.memset(tiny[:, 7:8], 0.0)

                CH = CHAIN_STEPS
                chain(dve.tensor_copy(st.rearrange("p a b -> p (a b)"),
                                      s_all[:, bass.ds(r, 1), :].rearrange("p o n -> p (o n)")), True)
                for half in range(2):
                    d = dve.max(v16[:, half, 0:8], st[:, half, :])
                chain(d, True)
                for half in range(2):
                    dve.max_index(ix16[:, half, 0:8], v16[:, half, 0:8], st[:, half, :])
                    d = dve.match_replace(st2[:, half, :], v16[:, half, 0:8], st[:, half, :], LOWEST)
                chain(d, True)
                for half in range(2):
                    d = dve.max(v16[:, half, 8:16], st2[:, half, :])
                chain(d, True)
                for half in range(2):
                    dve.max_index(ix16[:, half, 8:16], v16[:, half, 8:16], st2[:, half, :])
                chain(dve.tensor_tensor(cand, v16[:, 0, :].unsqueeze(2).to_broadcast([P, TOPK, TOPK]),
                                        v16[:, 1, None, :].to_broadcast([P, TOPK, TOPK]), ALU.add), True)
                flat = cand.rearrange("p a b -> p (a b)")
                chain(dve.max(top16[:, 0:8], flat), True)
                dve.max_index(pos16[:, 0, 0:8], top16[:, 0:8], flat)
                chain(dve.match_replace(cand2, top16[:, 0:8], flat, LOWEST), True)
                chain(dve.max(top16[:, 8:16], cand2), True)
                chain(dve.max_index(pos16[:, 0, 8:16], top16[:, 8:16], cand2))
                dve.tensor_scalar(pos16[:, 1, :], pos16[:, 0, :], 4, None, ALU.logical_shift_right)
                dve.tensor_copy(ix16f, ix16[:, :, :])
                dve.tensor_scalar(gates[:, bass.ds(r, 1), :].rearrange("p o n -> p (o n)"), top16, top16[:, 0:1],
                                  None, ALU.subtract)
                chain(dve.tensor_scalar(pos16[:, 2, :], pos16[:, 0, :], 15, None, ALU.bitwise_and))
                chain(dve.tensor_copy(pos_f, pos16[:, 1:3, :]))
                cols = iota[:, None, 0:TOPK].to_broadcast([P, TOPK, TOPK])
                for which, pick in enumerate((pick_a, pick_b)):
                    d = dve.tensor_tensor(pick, pos_f[:, which, :].unsqueeze(2).to_broadcast([P, TOPK, TOPK]),
                                          cols, ALU.is_equal)
                chain(d)
                for which, pick in enumerate((pick_a, pick_b)):
                    d = dve.tensor_tensor(pick, pick, ix16f[:, which, None, :].to_broadcast([P, TOPK, TOPK]),
                                          ALU.mult)
                chain(d)
                for pick, dst in ((pick_a, idx1), (pick_b, idx2)):
                    d = dve.tensor_reduce(dst[:, bass.ds(r, 1), :].rearrange("p o n -> p (o n)"), pick, AXX,
                                          ALU.add)
                chain(d)
                assert step[0] == CH
            count[0] = base + 2 * PEER_HEADS * CHAIN_STEPS
            dve.wait_ge(vec, count[0])
            dve.memset(tiny[:, 6:7], 0.0).then_inc(gate_in, 1)
            dve.wait_ge(gate_exp, 1)
            link(dve.tensor_reduce(gate_sum, gates, AXX, ALU.add))
            link(dve.reciprocal(gate_sum, gate_sum))
            dve.tensor_tensor(gates, gates, gate_sum.unsqueeze(2).to_broadcast([P, 16, TOPK]), ALU.mult)\
                .then_inc(sel_ready, 1)
            dve.wait_ge(selT_ready, 1)
            link(dve.tensor_copy(sel_T[:, 0:2, :], ps[:, 2, :].rearrange("p (a b) -> p a b", a=2)))
            dve.tensor_copy(sel_T[:, 2, :], ps[:, 3, 0:T]).then_inc(selT_copied, 1)
            dve.wait_ge(selT_copied, 1)

            def second_key(i, j):
                for t in range(2):
                    at_t = at(i, 8, 2 * j + t)
                    d = dve.tensor_scalar(oh2[:, j % 2, t, :], iota[:, :], sel_T[:, 1, bass.ds(at_t, 1)],
                                          sel_T[:, 2, bass.ds(at_t, 1)], ALU.is_equal, ALU.mult)
                d.then_inc(oh2_ready, 1)

            for j in range(4):
                if j >= 2:
                    dve.wait_ge(oh_used, j - 1)
                second_key(None, j)
            with dve.Fori(1, T // 8) as i:
                for j in range(4):
                    dve.wait_ge(oh_used, at(i, 4, j - 1))
                    second_key(i, j)

            def route(b0, i, per):
                dve.wait_ge(gemm_evac, at(i, per, B_UP + b0 + 1))
                dst = routed_v[:, b0, :] if i is None else \
                    routed_v[:, bass.ds(i * per + b0, 1), :].rearrange("p o t -> p (o t)")
                dve.tensor_tensor(dst, dst, gel[:, b0 % 2, :], ALU.mult).then_inc(routed, 1)

            dve.wait_ge(w_evac, T // 4)
            for j in range(4):
                lo(U_UP + j, S_UP + j, None, 4, 4)
                if j == 3:
                    route(0, None, 2)
            with dve.Fori(1, EXPERT_BLOCKS // 2) as i:
                for j in range(4):
                    lo(U_UP + j, S_UP + j, i, 4, 4)
                    if j % 2:
                        route(j // 2 - 1, i, 2)
            route(EXPERT_BLOCKS - 1, None, 2)

            def down(i):
                for j in range(4):
                    if j % 2 == 0:
                        src = routed_v[:, j // 2, :] if i is None else \
                            routed_v[:, bass.ds(i * 2 + j // 2, 1), :].rearrange("p o t -> p (o t)")
                        dve.wait_ge(at_hi, at(i, 2, j // 2 + 1))
                        dve.tensor_tensor(a_lo[:, j // 2, :], src, a_hi[:, j // 2, :].bitcast(F32), ALU.subtract)\
                            .then_inc(at_lo, 1)
                    lo(U_DOWN + j, S_DOWN + j, i, 4, 4)

            dve.wait_ge(routed, EXPERT_BLOCKS)
            down(None)
            with dve.Fori(1, EXPERT_BLOCKS // 2) as i:
                down(i)
            dve.wait_ge(ff_done, 1)
            for n in range(8):
                dve.tensor_copy(mixT[:, 2 * n:2 * n + 2, :], ps[:, n, :].rearrange("p (a b) -> p a b", a=2))\
                    .then_inc(ff_copied, 1)
            dve.wait_ge(ss_ready, 6)
            variance(ps[:, 7, 0:T], D, EPS, rs[:, :], var_ready)
            dve.wait_ge(rs_ready, 4)
            dve.wait_ge(x2_back, 16)
            for q in range(4):
                for kc in range(4 * q, 4 * q + 4):
                    d = dve.scalar_tensor_tensor(mixT[:, kc, :], mixT[:, kc, :], mod[:, 5, kc:kc + 1], rs[:, :],
                                                 ALU.mult, ALU.mult)
                link(d)
                s = slice(4 * q, 4 * q + 4)
                dve.tensor_tensor(mixT[:, s, :], mixT[:, s, :], xT[:, s, :], ALU.add).then_inc(out_ready, 1)


CHAIN_STEPS = 14


def kernel(x, c, w_ada, b_ada, g_pre_mix, g_post_mix, g_pre_ffn, g_post_ffn, w_in, lambda_q1, lambda_k1,
           lambda_q2, lambda_k2, g_subln, conv_w, conv_b, conv_ln_g, conv_ln_b, w_out, peer_wq, peer_k1,
           peer_k2, peer_u, peer_v):
    import numpy as np
    import concourse.bacc as bacc
    from concourse.bass_utils import run_bass_kernel_spmd

    def columns(v):
        return np.asarray(v).reshape(-1, P).T

    def blocks(w):
        w = np.asarray(w)
        return np.ascontiguousarray(w.reshape(KC, P, -1, P).transpose(2, 1, 0, 3)).reshape(-1, P, D)

    w_in_b = blocks(w_in[0])
    w_in_b = np.concatenate([w_in_b[24:40], w_in_b[0:24]])
    u = np.asarray(peer_u[0]).reshape(KEYS, KEYS, KC, P).transpose(0, 3, 2, 1)
    arrays = {
        "x": np.ascontiguousarray(np.asarray(x)[0].T.reshape(KC, P, T).transpose(1, 0, 2)).reshape(P, KC * T),
        "c": np.ascontiguousarray(columns(c)),
        "w_ada": np.asarray(w_ada)[0],
        "b_ada": np.ascontiguousarray(columns(b_ada)),
        "g_vecs": np.ascontiguousarray(np.stack([columns(g) for g in (g_pre_mix, g_post_mix, g_pre_ffn,
                                                                      g_post_ffn)], axis=1)),
        "w_in": w_in_b,
        "lambdas": np.stack([np.asarray(v)[0] for v in (lambda_q1, lambda_k1, lambda_q2, lambda_k2)]),
        "g_subln": np.ascontiguousarray(columns(g_subln)),
        "conv_w": np.ascontiguousarray(np.asarray(conv_w)[0].T.reshape(CONV_CHUNKS, P, TAPS).transpose(1, 0, 2)),
        "conv_vecs": np.ascontiguousarray(np.stack([columns(v) for v in (conv_b, conv_ln_g, conv_ln_b)], axis=1)),
        "w_out": blocks(w_out[0]),
        "peer_wq": blocks(peer_wq[0]),
        "peer_keys": np.stack([np.asarray(k)[0].T for k in (peer_k1, peer_k2)]),
        "peer_u": np.ascontiguousarray(u).reshape(KEYS, P, D),
        "peer_v": np.asarray(peer_v)[0].reshape(KEYS, P, D),
    }
    nc = bacc.Bacc("TRN2", target_bir_lowering=False, num_devices=1)
    aps = {n: nc.dram_tensor("in_" + n, a.shape, mybir.dt.from_np(a.dtype), kind="ExternalInput").ap()
           for n, a in arrays.items()}
    out = nc.dram_tensor("out_0", (P, KC * T), F32, kind="ExternalOutput").ap()
    build_block(nc, out=out, **aps)
    got = run_bass_kernel_spmd(nc, [{"in_" + n: a for n, a in arrays.items()}], core_ids=[0])
    y = got.results[0]["out_0"].reshape(P, KC, T).transpose(2, 1, 0).reshape(1, T, D)
    return np.ascontiguousarray(y)
```

```python
from contextlib import ExitStack
import math

import concourse.bass as bass
from concourse import mybir

P = 128
D = 2048
T = 256
KC = D // P
HEADS = 8
HEAD_DIM = 64
TAPS = 31
PAD = TAPS - 1
CONV_CHUNKS = 8
PEER_HEADS = 8
KEYS = 128
TOPK = 16
EPS = 1e-6
LAMBDA_INIT = 0.8 - 0.6 * math.exp(-0.3 * 0)
SCALE = 1.0 / math.sqrt(HEAD_DIM)
SLOPES = [2.0 ** (-8.0 * (h + 1.0) / HEADS) for h in range(HEADS)]
FAR = 1e30
LOWEST = -3e38

RAW = 4
WIDE = 8
UNIT = 1024
UCH = UNIT // P
IN_BLOCKS = 40
BLOCKS = D // P
EXPERT_BLOCKS = KEYS

EARLY = 2 * 2 * PEER_HEADS


def at(i, step, first):
    return first if i is None else i * step + first


STEPS = {"w": 1, "p": 2, "a": 1}


class Phase:

    def __init__(self, before, n, pattern, group=None, row=0, ring=RAW):
        assert len(pattern) % ring == 0
        self.ring, self.before = ring, before
        self.landings = before.landings_end if before else [0] * WIDE
        self.landings_end = [k + (n * len(pattern) // ring if place < ring else 0)
                             for place, k in enumerate(self.landings)]
        self.n, self.pattern, self.group, self.row = n, pattern, group, row
        self.u = before.u_end if before else 0
        self.first = {k: before.end[k] if before else 0 for k in "wpa"}
        self.per = len(pattern)
        self.each = {k: pattern.count(k) for k in "wpa"}
        self.u_end = self.u + n * self.per
        self.end = {k: self.first[k] + n * self.each[k] for k in "wpa"}
        self.s, self.s_per, self.s_end = (x["w"] + x["p"] for x in (self.first, self.each, self.end))
        self.block = self.s // 2

    def nth(self, j):
        same = "a" if self.pattern[j] == "a" else "wp"
        return sum(k in same for k in self.pattern[:j])

    def landed(self, j, i):
        return at(i, 16 * (self.per // self.ring), 16 * (self.landings[j % self.ring] + j // self.ring + 1))

    def user_before(self, j):
        if j >= self.ring:
            return self, 0, j - self.ring
        ph = self.before
        while ph and j >= ph.ring:
            ph = ph.before
        return ph and (ph, ph.n - 1, ph.per - ph.ring + j)

    def halves(self, n):
        places = [j for j, k in enumerate(self.pattern) if k != "a"]
        return places[2 * n:2 * n + 2]

    def done(self, j, i):
        kind = self.pattern[j]
        n = STEPS[kind]
        return at(i, n * self.each[kind], n * (self.first[kind] + self.pattern[:j].count(kind) + 1))


PH_SHIFT = Phase(None, KC // 4, "aaaaaaaa", 0, ring=WIDE)
PH_SCALE = Phase(PH_SHIFT, KC // 4, "aaaaaaaa", 1, ring=WIDE)
PH_GLU = Phase(PH_SCALE, BLOCKS // 4, "ppaappaa", 2, ring=WIDE)
PH_CONV = Phase(PH_GLU, BLOCKS // 4, "ppaappaa", 2, PH_GLU.n * 2, WIDE)
PH_QKV = Phase(PH_CONV, (IN_BLOCKS - BLOCKS) // 6, 2 * "ppappapp", 3, ring=WIDE)
PH_ATT = Phase(PH_QKV, (KC - 2 * PH_QKV.n) // 2, "aaaa", 3, PH_QKV.n * 2)
PH_OUT = Phase(PH_ATT, BLOCKS // 2, "wwaawwaa", 4)
PH_WQ = Phase(PH_OUT, BLOCKS // 2, "wwww")
PH_EARLY = Phase(PH_WQ, EARLY // 2, "pppp")
PH_GATE = Phase(PH_EARLY, KC // 2, "wwawwawwawwa", 5)
PH_UP = Phase(PH_GATE, (EXPERT_BLOCKS - EARLY) // 2 - 2 * PH_GATE.n, "wwww")
PH_DOWN = Phase(PH_UP, EXPERT_BLOCKS // 2, "wwww")
PHASES = [PH_SHIFT, PH_SCALE, PH_GLU, PH_CONV, PH_QKV, PH_ATT, PH_OUT, PH_WQ, PH_EARLY, PH_GATE, PH_UP, PH_DOWN]
B_UP = PH_EARLY.block
B_END = B_UP + EXPERT_BLOCKS

F32 = mybir.dt.float32
F32R = mybir.dt.float32r
U32 = mybir.dt.uint32
ALU = mybir.AluOpType
ACT = mybir.ActivationFunctionType
AXX = mybir.AxisListType.X


def build_block(nc, x, c, w_ada, b_ada, g_vecs, w_in, lambdas, g_subln, conv_w, conv_vecs,
                w_out, peer_wq, peer_keys, peer_u, peer_v, out):
    with ExitStack() as ctx:
        def sb(name, shape, dt=F32):
            return ctx.enter_context(nc.sbuf_tensor(name, shape, dt))

        def sem(name):
            return ctx.enter_context(nc.semaphore(name))

        big = sb("big", [P, KEYS * T])
        routed_v = big[:, :].rearrange("p (i t) -> p i t", t=T)
        routed_by_token = big[:, :].rearrange("p (i t) -> p t i", t=T)

        def region(start, *shape):
            n = int(math.prod(shape))
            v = big[:, start:start + n]
            if len(shape) == 2:
                v = v.rearrange("p (a b) -> p a b", b=shape[1])
            if len(shape) == 3:
                v = v.rearrange("p (a b c) -> p a b c", b=shape[1], c=shape[2])
            return v

        xT = region(0, KC, T)
        hT = region(4096, KC, T)
        proj = region(8192, IN_BLOCKS, T)
        convT = region(8192, CONV_CHUNKS, T)
        conv_sq = region(10240, CONV_CHUNKS, T)
        mixT = region(8192, KC, T)
        squares = region(12288, KC, T)
        acc_even = region(18432, D)
        acc_odd = region(6144, D)
        head_row = region(20480, HEADS, P)
        head_col = region(21504, HEADS, HEADS)
        upad = region(22528, CONV_CHUNKS, T + PAD)
        oT = region(24832, HEADS, T)
        v_tok = region(26880, 2 * HEADS, P)
        probs = region(28928, 2, 2, 384)
        aT = region(30464, 2, 384)
        distm = region(31232, 384)
        conv_wt = region(31616, CONV_CHUNKS, TAPS)
        conv_v = region(31864, 3, CONV_CHUNKS)
        lam_in = region(31888, 4, HEAD_DIM)
        stat = region(32144, 2, T)
        keysT = region(16384, 2, KEYS)
        rs = region(16640, T)
        o_sq = region(4096, HEADS, T)
        o_rs = region(31888, T)
        s_all = region(12288, 16, 2 * KEYS)
        rt = 22528
        h_full = squares
        st = region(rt, 2, KEYS)
        st2 = region(rt + 256, 2, KEYS)
        cand = region(rt + 512, TOPK, TOPK)
        cand2 = region(rt + 768, TOPK * TOPK)
        pick_a = region(rt + 1024, TOPK, TOPK)
        pick_b = region(rt + 1280, TOPK, TOPK)
        v16 = region(rt + 1536, 2, TOPK)
        top16 = region(rt + 1568, TOPK)
        ix16f = region(rt + 1584, 2, TOPK)
        pos_f = region(rt + 1616, 2, TOPK)
        gates = region(rt + 1664, 16, TOPK)
        gate_sum = region(rt + 1920, 16)
        idx1 = region(rt + 2048, 16, TOPK)
        idx2 = region(rt + 2304, 16, TOPK)
        ix16 = sb("ix16", [P, 2, TOPK], U32)
        pos16 = sb("pos16", [P, 3, TOPK], U32)

        a_hi = sb("a_hi", [P, KC, T], F32R)
        a_lo = sb("a_lo", [P, KC, T], F32R)
        raw = sb("raw", [P, RAW, UNIT])
        ring = [raw[:, n, :] for n in range(RAW)] + \
            [region(26880 + n * UNIT, UNIT) for n in range(WIDE - RAW)]
        w_hi = sb("w_hi", [P, 2, UNIT], F32R)
        w_lo = sb("w_lo", [P, 2, UNIT], F32R)

        ones = sb("ones", [P, P])
        ident = sb("ident", [P, P])
        iota = sb("iota", [P, P])
        cT = sb("cT", [P, KC])
        mod_b = sb("mod_b", [P, 6 * KC])
        mod = sb("mod", [P, 6, KC])
        gv = sb("gv", [P, 4, KC])
        gsub = sb("gsub", [P, 1])
        scratch = sb("scratch", [P, 9 * T])
        sel_T = scratch[:, 0:3 * T].rearrange("p (a b) -> p a b", b=T)
        acc_last = scratch[:, 0:D]
        gel = sb("gel", [P, 2, T])

        def four_rows(v):
            return v.rearrange("p (t k) -> p t k", k=P)

        oh1 = (four_rows(raw[:, 2, 0:512]), four_rows(raw[:, 3, 0:512]), four_rows(scratch[:, 768:1280]),
               four_rows(scratch[:, 1792:2304]))
        oh2 = (four_rows(raw[:, 2, 512:1024]), four_rows(raw[:, 3, 512:1024]), four_rows(scratch[:, 1280:1792]),
               four_rows(gel[:, :, :].rearrange("p a b -> p (a b)")))
        tiny = sb("tiny", [P, 32])
        lam_sum, lam_exp, neg_lam = tiny[:, 0:2], tiny[:, 2:4], tiny[:, 4:5]
        mx = [tiny[:, 8:12], tiny[:, 12:16]]
        sums = [tiny[:, 16:20], tiny[:, 20:24]]
        rcp = [tiny[:, 24:28], tiny[:, 28:32]]

        ps = ctx.enter_context(nc.psum_tensor("ps", [P, 8, 512], F32))
        x_saved = nc.dram_tensor("x_saved", (P, KC * T), F32, kind="Internal").ap()

        landed = [sem(f"landed{j}") for j in range(WIDE)]
        x_in, small_in = sem("x_in"), sem("small_in")
        hi_ready, lo_ready, split_used, ada_used = (sem("hi_ready"), sem("lo_ready"), sem("split_used"),
                                                    sem("ada_used"))
        lo_pool = sem("lo_pool")
        unit_done = {"w": lo_ready, "p": lo_pool, "a": ada_used}
        gemm_evac = sem("gemm_evac")
        consts, pool = sem("consts"), sem("pool")
        vec, s_first = sem("vec"), sem("s_first")
        sq_ready, ss_ready, var_ready, rs_ready = (sem("sq_ready"), sem("ss_ready"), sem("var_ready"),
                                                   sem("rs_ready"))
        silu_c, mod_sum, mod_ready = sem("silu_c"), sem("mod_sum"), sem("mod_ready")
        t_ready, h_hi, h_made, h_ready = sem("t_ready"), sem("h_hi"), sem("h_made"), sem("h_ready")
        glu_ready, tap = sem("glu_ready"), sem("tap")
        s_ready, s_read, neg_max, exp_done = sem("s_ready"), sem("s_read"), sem("neg_max"), sem("exp_done")
        a_ready, aT_ready, aT_copied = sem("a_ready"), sem("aT_ready"), sem("aT_copied")
        o_ready, o_copied, vt_ready, vt_copied = sem("o_ready"), sem("o_copied"), sem("vt_ready"), sem("vt_copied")
        lam_dots, lam_e = sem("lam_dots"), sem("lam_e")
        conv_stat = sem("conv_stat")
        conv_sq_ready, z_ready, y_ready = sem("conv_sq_ready"), sem("z_ready"), sem("y_ready")
        o_sq_ready, o_ss, o_var = sem("o_sq_ready"), sem("o_ss"), sem("o_var")
        o_root, o_spread = sem("o_root"), sem("o_spread")
        conv_var, conv_rs, conv_n = sem("conv_var"), sem("conv_rs"), sem("conv_n")
        x2_ready, x2_saved, x2_back = sem("x2_ready"), sem("x2_saved"), sem("x2_back")
        sc_ready, sc_copied = sem("sc_ready"), sem("sc_copied")
        gate_in, gate_exp, sel_ready, selT_ready, selT_copied = (sem("gate_in"), sem("gate_exp"),
                                                                 sem("sel_ready"), sem("selT_ready"),
                                                                 sem("selT_copied"))
        oh_ready, gated_act, gated_pool, oh_used = (sem("oh_ready"), sem("gated_act"), sem("gated_pool"),
                                                    sem("oh_used"))
        w_evac, w_early, routed = sem("w_evac"), sem("w_early"), sem("routed")
        at_hi, at_lo, ff_copied, out_ready, out_done = (sem("at_hi"), sem("at_lo"), sem("ff_copied"),
                                                        sem("out_ready"), sem("out_done"))

        ada = w_ada.rearrange("(k p) n -> k p n", p=P)
        N_SMALL = 7
        block = ctx.enter_context(nc.Block())

        def low_part(engine, ph, j, i):
            s = ph.s + ph.nth(j)
            engine.wait_ge(hi_ready, at(i, ph.s_per, s + 1))
            steps = STEPS[ph.pattern[j]]
            for n in range(steps):
                part = slice(n * UNIT // steps, (n + 1) * UNIT // steps)
                engine.tensor_tensor(w_lo[:, s % 2, part], ring[j % ph.ring][:, part], w_hi[:, s % 2, part].bitcast(F32),
                                     ALU.subtract).then_inc(unit_done[ph.pattern[j]], 1)

        @block.sync
        def _(sp):
            def slot_free(ph, j, i):
                if i is None:
                    if not ph.user_before(j):
                        return
                    before, it, place = ph.user_before(j)
                    count = before.done(place, it)
                elif j >= ph.ring:
                    before, place, count = ph, j - ph.ring, ph.done(j - ph.ring, i)
                else:
                    before, place = ph, j - ph.ring + ph.per
                    steps = STEPS[ph.pattern[place]] * ph.each[ph.pattern[place]]
                    count = at(i, steps, ph.done(place, None) - steps)
                sp.wait_ge(unit_done[before.pattern[place]], count)

            def bring(ph, i, w, block0=0):
                for j, kind in enumerate(ph.pattern):
                    nth = ph.nth(j)
                    slot_free(ph, j, i)
                    per, src = (ph.each["a"], ada) if kind == "a" else (ph.s_per, w)
                    half = slice((nth % 2) * UNIT, (nth % 2 + 1) * UNIT)
                    if kind == "a":
                        half = slice(ph.group * D + half.start, ph.group * D + half.stop)
                    row = nth // 2 + (ph.row if kind == "a" else block0)
                    if i is None:
                        src = src[row, :, half]
                    else:
                        src = src[bass.ds(i * (per // 2) + row, 1), :, half].rearrange("o p n -> (o p) n")
                    if ph is PH_GATE and i is None and j in (2, 3):
                        sp.wait_ge(oh_used, T // 4)
                    sp.dma_start(ring[j % ph.ring], src).then_inc(landed[j % ph.ring], 16)

            for ph, w, block0 in ((PH_SHIFT, None, 0), (PH_SCALE, None, 0), (PH_GLU, w_in, 0),
                                  (PH_CONV, w_in, PH_CONV.block), (PH_QKV, w_in, BLOCKS), (PH_ATT, None, 0), (PH_OUT, w_out, 0),
                                  (PH_WQ, peer_wq, 0), (PH_EARLY, peer_u, 0), (PH_GATE, peer_u, EARLY),
                                  (PH_UP, peer_u, EARLY + 4 * PH_GATE.n), (PH_DOWN, peer_v, 0)):
                bring(ph, None, w, block0)
                with sp.Fori(1, ph.n) as i:
                    bring(ph, i, w, block0)
            sp.wait_ge(at_lo, EXPERT_BLOCKS)
            sp.dma_start(xT.rearrange("p a b -> p (a b)"), x_saved).then_inc(x2_back, 16)
            for q in range(4):
                sp.wait_ge(out_ready, q + 1)
                sp.dma_start(out[:, q * 1024:(q + 1) * 1024],
                             mixT[:, 4 * q:4 * q + 4, :].rearrange("p a b -> p (a b)")).then_inc(out_done, 16)
            sp.wait_ge(out_done, 64)

        @block.gpsimd
        def _(gp):
            gp.memset(ones[:, :], 1.0).then_inc(consts, 1)
            gp.memset(ident[:, :], 0.0).then_inc(pool, 1)
            gp.wait_ge(pool, 1)
            gp.affine_select(out=ident[:, :], in_=ident[:, :], compare_op=ALU.not_equal, fill=1.0, base=0,
                             pattern=[[-1, P]], channel_multiplier=1).then_inc(consts, 1)
            gp.iota(iota[:, :], pattern=[[1, P]], base=0, channel_multiplier=0,
                    allow_small_or_imprecise_dtypes=True).then_inc(consts, 1)
            gp.iota(distm[:, 0:128], pattern=[[-1, 128]], base=0, channel_multiplier=1,
                    allow_small_or_imprecise_dtypes=True).then_inc(pool, 1)
            gp.iota(distm[:, 128:384], pattern=[[-1, 256]], base=128, channel_multiplier=1,
                    allow_small_or_imprecise_dtypes=True).then_inc(pool, 1)
            gp.wait_ge(pool, 3)
            gp.affine_select(out=distm[:, 0:128], in_=distm[:, 0:128], compare_op=ALU.is_ge, fill=FAR, base=0,
                             pattern=[[-1, 128]], channel_multiplier=1).then_inc(consts, 1)
            gp.affine_select(out=distm[:, 128:384], in_=distm[:, 128:384], compare_op=ALU.is_ge, fill=FAR,
                             base=128, pattern=[[-1, 256]], channel_multiplier=1).then_inc(consts, 1)
            gp.memset(head_row, 0.0).then_inc(pool, 1)
            gp.memset(head_col, 0.0).then_inc(pool, 1)
            gp.wait_ge(pool, 5)
            gp.affine_select(out=head_row, in_=head_row, compare_op=ALU.not_equal, fill=1.0, base=0,
                             pattern=[[-1, HEADS], [0, P]], channel_multiplier=1).then_inc(consts, 1)
            gp.affine_select(out=head_col, in_=head_col, compare_op=ALU.not_equal, fill=1.0, base=0,
                             pattern=[[1, HEADS], [-1, HEADS]], channel_multiplier=0).then_inc(consts, 1)
            gp.memset(upad[:, :, 0:PAD], 0.0).then_inc(consts, 1)
            for ph in (PH_GLU, PH_CONV, PH_QKV, PH_EARLY):
                with gp.Fori(0, ph.n) as i:
                    for j, kind in enumerate(ph.pattern):
                        if kind == "p":
                            low_part(gp, ph, j, i)
            gp.wait_ge(selT_copied, 1)
            with gp.Fori(0, T // 16) as i:
                for j in range(4):
                    gp.wait_ge(oh_ready, i * 4 + (j + 1))
                    gp.tensor_tensor(oh2[j][:, 2:4, :], oh2[j][:, 2:4, :],
                                     sel_T[:, 2, bass.ds(i * 16 + (4 * j + 2), 2)].unsqueeze(2)
                                     .to_broadcast([P, 2, P]), ALU.mult).then_inc(gated_pool, 1)

        @block.scalar
        def _(act):
            act.dma_start(xT.rearrange("p a b -> p (a b)"), x).then_inc(x_in, 16)
            act.dma_start(cT[:, :], c).then_inc(small_in, 16)
            act.dma_start(mod_b[:, :], b_ada).then_inc(small_in, 16)
            act.dma_start(gv[:, :, :], g_vecs).then_inc(small_in, 16)
            act.dma_start(gsub[:, :], g_subln).then_inc(small_in, 16)
            act.dma_start(conv_wt, conv_w).then_inc(small_in, 16)
            act.dma_start(conv_v, conv_vecs).then_inc(small_in, 16)
            act.dma_start(lam_in, lambdas.partition_broadcast(P)).then_inc(small_in, 16)
            act.wait_ge(small_in, 16 * N_SMALL)
            act.activation(cT[:, :], cT[:, :], ACT.Silu).then_inc(silu_c, 1)
            act.wait_ge(x_in, 16)
            act.activation(squares, xT, ACT.Square).then_inc(sq_ready, 1)
            act.wait_ge(lam_dots, 2)
            act.activation(lam_exp, lam_sum, ACT.Exp).then_inc(lam_e, 1)

            def root(n):
                act.wait_ge(var_ready, n)
                act.activation(rs, rs, ACT.Sqrt).then_inc(rs_ready, 1)

            def modulated(shift, n):
                for kc in range(KC):
                    act.wait_ge(t_ready, n + kc + 1)
                    act.activation(a_hi[:, kc, :], hT[:, kc, :], ACT.Identity, bias=mod[:, shift, kc:kc + 1])\
                        .then_inc(h_hi, 1)
                    act.activation(h_full[:, kc, :], hT[:, kc, :], ACT.Identity, bias=mod[:, shift, kc:kc + 1])\
                        .then_inc(h_made, 1)

            root(1)
            modulated(0, 0)

            def hi(ph, j, i):
                s = ph.s + ph.nth(j)
                act.wait_ge(landed[j % ph.ring], ph.landed(j, i))
                if s >= 2 or i is not None:
                    act.wait_ge(split_used, at(i, ph.s_per, s - 1))
                act.activation(w_hi[:, s % 2, :], ring[j % ph.ring], ACT.Copy).then_inc(hi_ready, 1)

            def chunk(buf, b0, i, per):
                if i is None:
                    return buf[:, b0, :]
                return buf[:, bass.ds(i * per + b0, 1), :].rearrange("p o t -> p (o t)")

            def whole(b0, i, per):
                act.wait_ge(split_used, at(i, 2 * per, 2 * b0 + 2))

            def evac(buf, first_block):
                def put(b0, i, per):
                    whole(b0, i, per)
                    act.activation(chunk(buf, b0 - first_block, i, per), ps[:, b0 % 2, 0:T], ACT.Copy)\
                        .then_inc(gemm_evac, 1)
                return put

            def split_and_put(ph, i, put, first=False, skip=0):
                for j, kind in enumerate(ph.pattern[skip:], skip):
                    if kind != "a":
                        hi(ph, j, i)
                        if ph.nth(j) % 2 and not (first and ph.nth(j) == 1):
                            put(ph.block + ph.nth(j) // 2 - 1, i, ph.s_per // 2)

            def run(ph, put, start=0, first=False):
                if first:
                    split_and_put(ph, None, put, True)
                    start = 1
                with act.Fori(start, ph.n) as i:
                    split_and_put(ph, i, put)

            to_proj = evac(proj, 0)

            def to_glu(b0, i, per):
                if b0 % 2 == 0:
                    to_proj(b0, i, per)
                    return
                whole(b0, i, per)
                act.activation(chunk(proj, b0, i, per), ps[:, b0 % 2, 0:T], ACT.Sigmoid).then_inc(gemm_evac, 1)

            run(PH_GLU, to_glu, first=True)
            run(PH_CONV, to_glu)
            hi(PH_QKV, 0, None)
            hi(PH_QKV, 1, None)
            to_glu(BLOCKS - 1, None, 1)
            split_and_put(PH_QKV, None, to_proj, skip=2)
            run(PH_QKV, to_proj, start=1)
            to_proj(IN_BLOCKS - 1, None, 1)

            def exps(h):
                act.wait_ge(neg_max, h + 1)
                for m in range(2):
                    for qb, (a, b) in enumerate(((0, 128), (128, 384))):
                        done = act.activation(probs[:, h % 2, m, a:b], probs[:, h % 2, m, a:b], ACT.Exp,
                                              bias=mx[h % 2][:, 2 * m + qb:2 * m + qb + 1], scale=SCALE,
                                              accum_out=sums[h % 2][:, 2 * m + qb:2 * m + qb + 1])
                done.then_inc(exp_done, 1)

            exps(0)
            exps(1)
            for h in range(HEADS):
                act.wait_ge(aT_ready, h + 1)
                if h >= 2:
                    act.wait_ge(o_ready, h - 1)
                act.activation(aT[:, h % 2, :], ps[:, 0, 0:384], ACT.Copy).then_inc(aT_copied, 1)
                act.wait_ge(o_ready, h + 1)
                act.activation(oT[:, h, :], ps[:, 1, 0:T], ACT.Copy).then_inc(o_copied, 1)
                if h + 2 < HEADS:
                    exps(h + 2)
                act.wait_ge(o_copied, h + 1)
                act.activation(o_sq[:, h, :], oT[:, h, :], ACT.Square).then_inc(o_sq_ready, 1)
                if h == 2:
                    act.wait_ge(conv_stat, 1)
                    act.activation(conv_sq, convT, ACT.Square).then_inc(conv_sq_ready, 1)
            act.dma_start(keysT[:, 0, :], peer_keys[0]).then_inc(small_in, 16)
            act.dma_start(keysT[:, 1, :], peer_keys[1]).then_inc(small_in, 16)
            act.wait_ge(conv_var, 1)
            act.activation(stat[:, 1, :], stat[:, 1, :], ACT.Sqrt).then_inc(conv_rs, 1)
            act.wait_ge(conv_n, 1)
            for ch in range(CONV_CHUNKS):
                act.activation(convT[:, ch, :], convT[:, ch, :], ACT.Silu, bias=conv_v[:, 2, ch:ch + 1],
                               scale=conv_v[:, 1, ch:ch + 1]).then_inc(z_ready, 1)
            act.wait_ge(o_var, 1)
            act.activation(o_rs[0:HEADS, :], o_rs[0:HEADS, :], ACT.Sqrt).then_inc(o_root, 1)
            for n in range(4):
                act.wait_ge(z_ready, 2 * n + 2)
                act.activation(a_hi[:, 2 * n:2 * n + 2, :], convT[:, 2 * n:2 * n + 2, :], ACT.Copy).then_inc(h_hi, 1)
            for n in range(4):
                act.wait_ge(y_ready, n + 1)
                act.activation(a_hi[:, 8 + 2 * n:10 + 2 * n, :], oT[:, 2 * n:2 * n + 2, :], ACT.Copy)\
                    .then_inc(h_hi, 1)

            mix_evac = evac(mixT, PH_OUT.block)

            def mix_out(b0, i, per):
                mix_evac(b0, i, per)
                act.wait_ge(gemm_evac, at(i, per, b0 + 1))
                act.activation(chunk(squares, b0 - PH_OUT.block, i, per),
                               chunk(mixT, b0 - PH_OUT.block, i, per), ACT.Square).then_inc(sq_ready, 1)

            for j in range(2):
                hi(PH_OUT, j, None)
            act.wait_ge(h_ready, KC + 8)
            for j in range(2, PH_OUT.per):
                if PH_OUT.pattern[j] == "w":
                    hi(PH_OUT, j, None)
            mix_out(PH_OUT.block, None, 1)
            run(PH_OUT, mix_out, start=1)
            mix_out(PH_WQ.block - 1, None, 1)
            root(2)
            for q in range(4):
                act.wait_ge(x2_ready, q + 1)
                act.activation(squares[:, 4 * q:4 * q + 4, :], xT[:, 4 * q:4 * q + 4, :], ACT.Square)\
                    .then_inc(sq_ready, 1)
            act.dma_start(x_saved, xT.rearrange("p a b -> p (a b)")).then_inc(x2_saved, 16)
            root(3)
            modulated(3, KC)

            to_q = evac(mixT, PH_WQ.block)
            run(PH_WQ, to_q, first=True)
            to_q(PH_EARLY.block - 1, None, 1)
            for n in range(8):
                act.wait_ge(sc_ready, n + 1)
                act.activation(s_all[:, 2 * n:2 * n + 2, :], ps[:, 2 + n % 2, :].rearrange("p (a b) -> p a b", a=2),
                               ACT.Copy).then_inc(sc_copied, 1)

            def gelu_stays(b0, i, per):
                whole(b0, i, per)
                act.activation(chunk(routed_v, b0 - B_UP, i, per), ps[:, b0 % 2, 0:T], ACT.Gelu)\
                    .then_inc(gemm_evac, 1)

            act.wait_ge(x2_saved, 16)
            run(PH_EARLY, gelu_stays, first=True)
            gelu_stays(PH_GATE.block - 1, None, 1)
            act.wait_ge(gate_in, 1)
            act.activation(gates, gates, ACT.Exp).then_inc(gate_exp, 1)

            def gated(i, j):
                act.wait_ge(oh_ready, at(i, 4, j + 1))
                for t in range(2):
                    d = act.activation(oh2[j][:, t, :], oh2[j][:, t, :], ACT.Copy,
                                       scale=sel_T[:, 2, bass.ds(at(i, 16, 4 * j + t), 1)])
                d.then_inc(gated_act, 1)

            def put_weights(i, j):
                act.wait_ge(oh_used, at(i, 4, j + 1))
                act.activation(routed_by_token[:, bass.ds(at(i, 16, 4 * j), 4), EARLY:],
                               ps[:, 2 + j % 4, :].rearrange("p (a b) -> p a b", a=4)[:, :, EARLY:], ACT.Copy)\
                    .then_inc(w_evac, 1)

            act.wait_ge(selT_copied, 1)
            for j in range(4):
                if j >= 2:
                    put_weights(None, j - 2)
                gated(None, j)
            with act.Fori(1, T // 16) as i:
                for j in range(4):
                    put_weights(i, j - 2)
                    gated(i, j)
            put_weights(None, T // 4 - 2)
            put_weights(None, T // 4 - 1)

            def gelu(b0, i, per):
                whole(b0, i, per)
                rel = b0 - PH_GATE.block
                if rel >= 2 or i is not None:
                    act.wait_ge(routed, at(i, per, rel - 1))
                act.activation(gel[:, b0 % 2, :], ps[:, b0 % 2, 0:T], ACT.Gelu).then_inc(gemm_evac, 1)

            act.wait_ge(w_early, T // 4)
            run(PH_GATE, gelu, first=True)
            run(PH_UP, gelu)
            gelu(B_END - 1, None, 1)

            def down(i):
                for j in range(4):
                    if j % 2 == 0:
                        act.wait_ge(split_used, at(i, 4, PH_DOWN.s + j - 2))
                        act.activation(a_hi[:, j // 2, :], chunk(routed_v, j // 2, i, 2), ACT.Copy)\
                            .then_inc(at_hi, 1)
                    hi(PH_DOWN, j, i)

            act.wait_ge(split_used, PH_DOWN.s)
            act.wait_ge(routed, EXPERT_BLOCKS - EARLY)
            down(None)
            with act.Fori(1, PH_DOWN.n) as i:
                down(i)
            for n in range(8):
                act.wait_ge(ff_copied, n + 1)
                act.activation(squares[:, 2 * n:2 * n + 2, :], mixT[:, 2 * n:2 * n + 2, :], ACT.Square)\
                    .then_inc(sq_ready, 1)
            root(4)

        @block.tensor
        def _(pe):
            def sum_squares(counts):
                for kc in range(KC):
                    pe.wait_ge(sq_ready, counts[kc])
                    done = pe.matmul(ps[:, 7, 0:T], ones[:, :], squares[:, kc, :], start=kc == 0, stop=kc == KC - 1)
                done.then_inc(ss_ready, 1)

            def modulation(group):
                acc = (acc_even, acc_odd, acc_even, acc_odd, acc_even, acc_last)[group]
                for dc in range(KC):
                    done = pe.matmul(ps[:, 6, group * KC + dc:group * KC + dc + 1], acc[:, dc * P:(dc + 1) * P],
                                     ones[:, 0:1], start=True, stop=True)
                done.then_inc(mod_sum, 1)

            def product(ph, n, i, chunks=None):
                b = ph.block + n
                if b >= 2 or i is not None:
                    pe.wait_ge(gemm_evac, at(i, ph.s_per // 2, b - 1))
                for half in range(2):
                    place = ph.halves(n)[half]
                    steps = STEPS[ph.pattern[place]]
                    for k in range(UCH):
                        kc = half * UCH + k
                        if k * steps % UCH == 0:
                            pe.wait_ge(unit_done[ph.pattern[place]],
                                       ph.done(place, i) - (steps - 1 - k * steps // UCH))
                        if chunks is not None:
                            pe.wait_ge(h_ready, chunks[kc])
                        for m, (w, a) in enumerate(((w_hi, a_hi), (w_hi, a_lo), (w_lo, a_hi))):
                            done = pe.matmul(ps[:, b % 2, 0:T], w[:, half, k * P:(k + 1) * P], a[:, kc, :],
                                             start=kc == 0 and m == 0, stop=kc == KC - 1 and m == 2)
                    done.then_inc(split_used, 1)

            def run(ph, chunks=None, after=None):
                if chunks:
                    for n in range(ph.s_per // 2):
                        product(ph, n, None, chunks if n == 0 else None)
                        if after:
                            after(n, None)
                with pe.Fori(1 if chunks else 0, ph.n) as i:
                    for n in range(ph.s_per // 2):
                        product(ph, n, i)
                        if after:
                            after(n, i)

            pe.wait_ge(consts, 8)
            sum_squares([1] * KC)
            pe.wait_ge(ada_used, PH_SHIFT.end["a"])
            modulation(0)
            pe.wait_ge(ada_used, PH_SCALE.end["a"])
            modulation(1)
            run(PH_GLU, chunks=[kc + 1 for kc in range(KC)])
            run(PH_CONV)
            run(PH_QKV)

            pe.wait_ge(gemm_evac, IN_BLOCKS)

            def scores(h):
                if h >= 2:
                    pe.wait_ge(s_read, h - 1)
                q, k = proj[:, 16 + h, :], proj[:, 24 + h, :]
                for m in range(2):
                    r = slice(64 * m, 64 * m + 64)
                    bank = 2 + 2 * (h % 2) + m
                    pe.matmul(ps[:, bank, 0:128], q[r, 0:128], k[r, 0:128], start=True, stop=True)
                    done = pe.matmul(ps[:, bank, 128:384], q[r, 128:256], k[r, :], start=True, stop=True)
                done.then_inc(s_ready, 1)

            scores(0)
            scores(1)
            pe.wait_ge(ada_used, PH_CONV.end["a"])
            modulation(2)
            for n in range(4):
                if n >= 2:
                    pe.wait_ge(vt_copied, n - 1)
                for j in range(4):
                    done = pe.transpose(ps[:, 7 * (n % 2), j * P:(j + 1) * P],
                                        proj[:, 32 + 2 * n + j // 2, (j % 2) * P:(j % 2 + 1) * P], ident[:, :])
                done.then_inc(vt_ready, 1)

            def over_channels(src, ready):
                pe.wait_ge(*ready)
                for ch in range(CONV_CHUNKS):
                    done = pe.matmul(ps[:, 7, 0:T], ones[:, :], src[:, ch, :], start=ch == 0,
                                     stop=ch == CONV_CHUNKS - 1)
                done.then_inc(ss_ready, 1)

            for h in range(HEADS):
                pe.wait_ge(a_ready, h + 1)
                pe.wait_ge(vt_copied, 4)
                if h >= 1:
                    pe.wait_ge(aT_copied, h)
                for j in range(3):
                    done = pe.transpose(ps[:, 0, j * P:(j + 1) * P], probs[:, h % 2, 0, j * P:(j + 1) * P],
                                        ident[:, :])
                done.then_inc(aT_ready, 1)
                if h + 2 < HEADS:
                    scores(h + 2)
                pe.wait_ge(aT_copied, h + 1)
                if h >= 1:
                    pe.wait_ge(o_copied, h)
                pe.matmul(ps[:, 1, 0:128], v_tok[:, 2 * h, :], aT[:, h % 2, 0:128], start=True, stop=True)
                pe.matmul(ps[:, 1, 128:256], v_tok[:, 2 * h, :], aT[:, h % 2, 128:256], start=True, stop=False)
                pe.matmul(ps[:, 1, 128:256], v_tok[:, 2 * h + 1, :], aT[:, h % 2, 256:384], start=False,
                          stop=True).then_inc(o_ready, 1)
                if h == 0:
                    over_channels(convT, (tap, TAPS * CONV_CHUNKS))
                if h == 3:
                    over_channels(conv_sq, (conv_sq_ready, 1))
                if h == 6:
                    pe.wait_ge(mod_ready, 2)
                    pe.wait_ge(ada_used, PH_ATT.end["a"])
                    modulation(3)
            pe.wait_ge(conv_var, 1)
            for h in range(HEADS):
                pe.wait_ge(o_sq_ready, h + 1)
                done = pe.matmul(ps[0:HEADS, 7, 0:T], head_col[:, h, :], o_sq[:, h, :], start=h == 0,
                                 stop=h == HEADS - 1)
            done.then_inc(o_ss, 1)
            pe.wait_ge(o_root, 1)
            for h in range(HEADS):
                done = pe.matmul(ps[:, 2 + h // 2, (h % 2) * T:(h % 2 + 1) * T], head_row[0:HEADS, h, :],
                                 o_rs[0:HEADS, :], start=True, stop=True)
                if h % 2:
                    done.then_inc(o_spread, 1)

            def mix_sum(b, i):
                pe.wait_ge(sq_ready, at(i, 2, b + 2))
                src = squares[:, b, :] if i is None else \
                    squares[:, bass.ds(i * 2 + b, 1), :].rearrange("p o t -> p (o t)")
                return pe.matmul(ps[:, 7, 0:T], ones[:, :], src, start=i is None and b == 0, stop=False,
                                 skip_group_check=True)

            def behind(n, i):
                if n or i is not None:
                    mix_sum(n - 1, i)

            y_chunks = [KC + kc // 2 + 1 for kc in range(KC)]
            run(PH_OUT, chunks=y_chunks, after=behind)
            pe.wait_ge(ada_used, PH_OUT.end["a"])
            modulation(4)
            mix_sum(BLOCKS - 1, None).then_inc(ss_ready, 1)
            sum_squares([KC + 2 + kc // 4 for kc in range(KC)])
            run(PH_WQ, chunks=[KC + 9 + kc for kc in range(KC)])

            pe.wait_ge(gemm_evac, B_UP)
            pe.wait_ge(small_in, 16 * (N_SMALL + 2))
            for n in range(8):
                if n >= 2:
                    pe.wait_ge(sc_copied, n - 1)
                for j in range(4):
                    r, half = 2 * n + j // 2, j % 2
                    tt, h = r // 8, r % 8
                    done = pe.matmul(ps[:, 2 + n % 2, j * KEYS:(j + 1) * KEYS],
                                     mixT[:, 2 * h + half, tt * P:(tt + 1) * P], keysT[:, half, :],
                                     start=True, stop=True)
                done.then_inc(sc_ready, 1)
            run(PH_EARLY)
            pe.wait_ge(sc_copied, 8)
            pe.wait_ge(sel_ready, 1)
            for n, src in enumerate((idx1, idx2, gates)):
                flat = src.rearrange("p r k -> p (r k)")
                for tt in range(2):
                    done = pe.transpose(ps[:, 2 + n // 2, (n % 2) * T + tt * P:(n % 2) * T + (tt + 1) * P],
                                        flat[:, tt * P:(tt + 1) * P], ident[:, :])
            done.then_inc(selT_ready, 1)

            def weights(i, j):
                pe.wait_ge(gated_act, at(i, 4, j + 1))
                pe.wait_ge(gated_pool, at(i, 4, j + 1))
                if i is not None:
                    pe.wait_ge(w_early, at(i, 4, j - 3))
                for t in range(4):
                    done = pe.matmul(ps[:, 2 + j, t * P:(t + 1) * P], oh2[j][:, t, :], oh1[j][:, t, :],
                                     start=True, stop=True)
                done.then_inc(oh_used, 1)

            pe.wait_ge(selT_copied, 1)
            for j in range(4):
                weights(None, j)
            with pe.Fori(1, T // 16) as i:
                for j in range(4):
                    weights(i, j)

            run(PH_GATE)
            pe.wait_ge(ada_used, PH_GATE.end["a"])
            modulation(5)
            run(PH_UP)

            def down(i):
                for j in range(4):
                    blk = j // 2
                    if j % 2 == 0:
                        pe.wait_ge(at_lo, at(i, 2, blk + 1))
                    pe.wait_ge(lo_ready, PH_DOWN.done(j, i))
                    for k in range(UCH):
                        dt = (j % 2) * UCH + k
                        for n, (w, a) in enumerate(((w_hi, a_hi), (w_hi, a_lo), (w_lo, a_hi))):
                            done = pe.matmul(ps[:, dt // 2, (dt % 2) * T:(dt % 2 + 1) * T],
                                             w[:, j % 2, k * P:(k + 1) * P], a[:, blk, :],
                                             start=i is None and blk == 0 and n == 0 and dt % 2 == 0,
                                             stop=False, skip_group_check=True)
                    done.then_inc(split_used, 1)

            pe.wait_ge(gemm_evac, B_END)
            pe.wait_ge(mod_ready, 4)
            down(None)
            with pe.Fori(1, PH_DOWN.n) as i:
                down(i)
            pe.wait_ge(ff_copied, 8)
            sum_squares([KC + 6 + kc // 2 for kc in range(KC)])

        @block.vector
        def _(dve):
            count = [0]

            def link(ins):
                count[0] += 1
                ins.then_inc(vec, 1)
                dve.wait_ge(vec, count[0])

            def bcast_t(v, n=KC):
                return v[:, None, :].to_broadcast([P, n, T])

            def inverse_variance(bank, n, dst, done):
                link(dve.tensor_scalar(dst, bank, 1.0 / n, EPS, ALU.mult, ALU.add))
                dve.reciprocal(dst, dst).then_inc(done, 1)

            dve.wait_ge(small_in, 16 * N_SMALL)
            for n in range(2):
                link(dve.tensor_tensor(lam_in[:, 2 * n, :], lam_in[:, 2 * n, :], lam_in[:, 2 * n + 1, :], ALU.mult))
                dve.tensor_reduce(lam_sum[:, n:n + 1], lam_in[:, 2 * n, :], AXX, ALU.add).then_inc(lam_dots, 1)
            link(dve.tensor_scalar(gsub[:, :], gsub[:, :], 1.0 - LAMBDA_INIT, None, ALU.mult))
            dve.wait_ge(lam_e, 1)
            link(dve.tensor_tensor(neg_lam, lam_exp[:, 1:2], lam_exp[:, 0:1], ALU.subtract))
            link(dve.tensor_scalar(neg_lam, neg_lam, -LAMBDA_INIT, None, ALU.add))
            dve.wait_ge(silu_c, 1)

            def ada_step(ph, j, i, acc):
                nth, unit = ph.nth(j), ring[j % ph.ring]
                dve.wait_ge(landed[j % ph.ring], ph.landed(j, i))
                dst = acc[:, (nth % 2) * UNIT:(nth % 2 + 1) * UNIT]
                if i is None and ph.row == 0 and nth < 2:
                    dve.tensor_scalar(dst, unit, cT[:, 0:1], None, ALU.mult).then_inc(ada_used, 1)
                    return
                dve.wait_ge(ada_used, at(i, ph.each["a"], ph.first["a"] + nth - 1))
                kc = at(i, ph.each["a"] // 2, ph.row + nth // 2)
                dve.scalar_tensor_tensor(dst, unit, cT[:, bass.ds(kc, 1)], dst, ALU.mult, ALU.add)\
                    .then_inc(ada_used, 1)

            def sums_of(ph, acc):
                for j in range(ph.per):
                    ada_step(ph, j, None, acc)
                with dve.Fori(1, ph.n) as i:
                    for j in range(ph.per):
                        ada_step(ph, j, i, acc)

            def lo(ph, j, i):
                low_part(dve, ph, j, i)

            def mod_add(a, b, *ready):
                if ready:
                    dve.wait_ge(*ready)
                link(dve.tensor_tensor(mod[:, a:b, :], ps[:, 6, a * KC:b * KC].rearrange("p (a b) -> p a b", b=KC),
                                       mod_b[:, a * KC:b * KC].rearrange("p (a b) -> p a b", b=KC), ALU.add))

            def scaled(group, g):
                dve.scalar_tensor_tensor(mod[:, group, :], mod[:, group, :], 1.0, gv[:, g, :], ALU.add, ALU.mult)\
                    .then_inc(mod_ready, 1)

            def modulated(scale, n_t, n_h):
                def t(kc):
                    dve.scalar_tensor_tensor(hT[:, kc, :], xT[:, kc, :], mod[:, scale, kc:kc + 1], rs, ALU.mult,
                                             ALU.mult).then_inc(t_ready, 1)
                for kc in range(3):
                    t(kc)
                for kc in range(KC):
                    dve.wait_ge(h_made, n_t + kc + 1)
                    dve.tensor_tensor(a_lo[:, kc, :], h_full[:, kc, :], a_hi[:, kc, :].bitcast(F32), ALU.subtract)\
                        .then_inc(h_ready, 1)
                    if kc + 3 < KC:
                        t(kc + 3)

            sums_of(PH_SHIFT, acc_even)
            dve.wait_ge(ss_ready, 1)
            inverse_variance(ps[:, 7, 0:T], D, rs, var_ready)
            sums_of(PH_SCALE, acc_odd)
            mod_add(0, 2, mod_sum, 2)
            scaled(1, 0)
            dve.wait_ge(mod_ready, 1)
            dve.wait_ge(rs_ready, 1)
            modulated(1, 0, 0)

            def mixed(ph, i, acc):
                for j, kind in enumerate(ph.pattern):
                    if kind == "w":
                        lo(ph, j, i)
                    if kind == "a":
                        ada_step(ph, j, i, acc)

            def glu(first, i):
                dve.wait_ge(gemm_evac, at(i, 2, 2 * first + 2))
                pair = [proj[:, bass.ds(at(i, 2, 2 * first + k), 1), :].rearrange("p o t -> p (o t)")
                        for k in range(2)]
                dst = upad[:, bass.ds(at(i, 1, first), 1), PAD:PAD + T].rearrange("p o t -> p (o t)")
                dve.tensor_tensor(dst, pair[0], pair[1], ALU.mult).then_inc(glu_ready, 1)

            def conv_tap(ch, j, ntap):
                if isinstance(j, int) and j == 0:
                    dve.tensor_scalar(chan(convT, ch), chan(upad, ch)[:, 0:T], wcol(ch, 0), bcol(ch), ALU.mult,
                                      ALU.add).then_inc(tap, 1)
                    return
                dve.wait_ge(tap, ntap)
                dve.scalar_tensor_tensor(chan(convT, ch), chan(upad, ch)[:, bass.ds(j, T)], wcol(ch, j),
                                         chan(convT, ch), ALU.mult, ALU.add).then_inc(tap, 1)

            def chan(buf, ch):
                if isinstance(ch, int):
                    return buf[:, ch, :]
                return buf[:, bass.ds(ch, 1), :].rearrange("p o t -> p (o t)")

            def wcol(ch, j):
                if isinstance(ch, int):
                    return conv_wt[:, ch, bass.ds(j, 1)]
                return conv_wt[:, bass.ds(ch, 1), j:j + 1].rearrange("p o t -> p (o t)")

            def bcol(ch):
                return conv_v[:, 0, ch:ch + 1] if isinstance(ch, int) else conv_v[:, 0, bass.ds(ch, 1)]

            mixed(PH_GLU, None, acc_even)
            with dve.Fori(1, PH_GLU.n) as i:
                mixed(PH_GLU, i, acc_even)
                glu(-1, i)
            mixed(PH_CONV, None, acc_even)
            glu(PH_GLU.n - 1, None)
            dve.wait_ge(glu_ready, 1)
            conv_tap(0, 0, 0)
            with dve.Fori(1, PH_CONV.n) as i:
                mixed(PH_CONV, i, acc_even)
                glu(PH_GLU.n - 1, i)
                for k in range(10):
                    conv_tap(0, i * 10 + (k - 9), i * 10 + (k - 9))

            def qkv(i):
                chunks = (1,) if i is None else (i * 2, i * 2 + 1)
                steps = [(ch, k, at(i, 2 * TAPS, k + (TAPS if i is None else n * TAPS)))
                         for n, ch in enumerate(chunks) for k in range(TAPS)]
                for j, kind in enumerate(PH_QKV.pattern):
                    if kind == "w":
                        lo(PH_QKV, j, i)
                    if kind == "a":
                        ada_step(PH_QKV, j, i, acc_odd)
                    for step in steps[j * len(steps) // PH_QKV.per:(j + 1) * len(steps) // PH_QKV.per]:
                        conv_tap(*step)

            qkv(None)
            glu(CONV_CHUNKS - 1, None)
            dve.wait_ge(glu_ready, CONV_CHUNKS)
            with dve.Fori(1, PH_QKV.n) as i:
                qkv(i)

            def head_scores(h):
                dve.wait_ge(s_ready, h + 1)
                if h >= 2:
                    dve.wait_ge(aT_ready, h - 1)
                for m in range(2):
                    done = dve.scalar_tensor_tensor(probs[:, h % 2, m, :], distm, -SLOPES[h] / SCALE,
                                                    ps[:, 2 + 2 * (h % 2) + m, 0:384], ALU.mult, ALU.add)
                    done.then_inc(s_read_m[m], 1)
                for m in range(2):
                    dve.wait_ge(s_read_m[m], h + 1)
                    for qb, (a, b) in enumerate(((0, 128), (128, 384))):
                        done = dve.tensor_reduce(mx[h % 2][:, 2 * m + qb:2 * m + qb + 1], probs[:, h % 2, m, a:b],
                                                 AXX, ALU.max)
                link(done)
                dve.tensor_scalar(mx[h % 2], mx[h % 2], -SCALE, None, ALU.mult).then_inc(neg_max, 1)

            s_read_m = (s_first, s_read)

            def head_combine(h):
                p, r = probs[:, h % 2], rcp[h % 2]
                dve.wait_ge(exp_done, h + 1)
                link(dve.reciprocal(r, sums[h % 2]))
                link(dve.tensor_scalar(r[:, 2:4], r[:, 2:4], neg_lam, None, ALU.mult))
                for qb, (a, b) in enumerate(((0, 128), (128, 384))):
                    done = dve.tensor_scalar(p[:, 1, a:b], p[:, 1, a:b], r[:, 2 + qb:3 + qb], None, ALU.mult)
                link(done)
                for qb, (a, b) in enumerate(((0, 128), (128, 384))):
                    done = dve.scalar_tensor_tensor(p[:, 0, a:b], p[:, 0, a:b], r[:, qb:qb + 1], p[:, 1, a:b],
                                                    ALU.mult, ALU.add)
                done.then_inc(a_ready, 1)

            head_scores(0)
            head_scores(1)
            mod_add(2, 3, mod_sum, 3)
            dve.tensor_tensor(mod[:, 2, :], mod[:, 2, :], gv[:, 1, :], ALU.mult).then_inc(mod_ready, 1)
            for n in range(4):
                dve.wait_ge(vt_ready, n + 1)
                dve.tensor_copy(v_tok[:, 4 * n:4 * n + 4, :],
                                ps[:, 7 * (n % 2), :].rearrange("p (a b) -> p a b", a=4)).then_inc(vt_copied, 1)
            for h in range(HEADS):
                head_combine(h)
                for j in range(3 * h, min(3 * h + 3, PH_ATT.n * PH_ATT.per)):
                    ada_step(PH_ATT, j % PH_ATT.per, j // PH_ATT.per, acc_odd)
                if h + 2 < HEADS:
                    head_scores(h + 2)
                if h == 1:
                    dve.wait_ge(ss_ready, 2)
                    link(dve.tensor_scalar(stat[:, 0, :], ps[:, 7, 0:T], 1.0 / (P * CONV_CHUNKS), None, ALU.mult))
                    dve.tensor_tensor(convT, convT, bcast_t(stat[:, 0, :], 8), ALU.subtract).then_inc(conv_stat, 1)
                if h == 5:
                    dve.wait_ge(ss_ready, 3)
                    inverse_variance(ps[:, 7, 0:T], P * CONV_CHUNKS, stat[:, 1, :], conv_var)
            dve.wait_ge(conv_rs, 1)
            dve.tensor_tensor(convT, convT, bcast_t(stat[:, 1, :], 8), ALU.mult).then_inc(conv_n, 1)
            dve.wait_ge(o_ss, 1)
            inverse_variance(ps[0:HEADS, 7, 0:T], P, o_rs[0:HEADS, :], o_var)
            def low_of(n, src):
                dve.wait_ge(h_hi, KC + n + 1)
                dve.tensor_tensor(a_lo[:, 2 * n:2 * n + 2, :], src, a_hi[:, 2 * n:2 * n + 2, :].bitcast(F32),
                                  ALU.subtract).then_inc(h_ready, 1)

            for n in range(4):
                low_of(n, convT[:, 2 * n:2 * n + 2, :])
            for n in range(4):
                dve.wait_ge(o_spread, n + 1)
                two = oT[:, 2 * n:2 * n + 2, :].rearrange("p a b -> p (a b)")
                dve.scalar_tensor_tensor(two, two, gsub[:, 0:1], ps[:, 2 + n, :], ALU.mult, ALU.mult)\
                    .then_inc(y_ready, 1)
            for n in range(4):
                dve.wait_ge(y_ready, n + 1)
                low_of(4 + n, oT[:, 2 * n:2 * n + 2, :])

            mixed(PH_OUT, None, acc_even)
            with dve.Fori(1, PH_OUT.n) as i:
                mixed(PH_OUT, i, acc_even)

            mod_add(3, 5, mod_sum, 5)
            scaled(4, 2)
            dve.wait_ge(ss_ready, 4)
            inverse_variance(ps[:, 7, 0:T], D, rs, var_ready)
            dve.wait_ge(rs_ready, 2)
            for q in range(4):
                for kc in range(4 * q, 4 * q + 4):
                    done = dve.scalar_tensor_tensor(mixT[:, kc, :], mixT[:, kc, :], mod[:, 2, kc:kc + 1], rs,
                                                    ALU.mult, ALU.mult)
                link(done)
                s = slice(4 * q, 4 * q + 4)
                dve.tensor_tensor(xT[:, s, :], xT[:, s, :], mixT[:, s, :], ALU.add).then_inc(x2_ready, 1)
            dve.wait_ge(ss_ready, 5)
            inverse_variance(ps[:, 7, 0:T], D, rs, var_ready)
            dve.wait_ge(rs_ready, 3)
            dve.wait_ge(mod_ready, 3)
            dve.wait_ge(x2_ready, 4)
            modulated(4, KC, KC + 8)

            with dve.Fori(0, PH_WQ.n) as i:
                for j in range(4):
                    lo(PH_WQ, j, i)

            base = count[0]
            with dve.Fori(0, 2 * PEER_HEADS) as r:
                step = [0]

                def chain(ins, before_max=False):
                    step[0] += 1
                    ins.then_inc(vec, 1)
                    dve.wait_ge(vec, r * CHAIN_STEPS + (base + step[0]))
                    if before_max:
                        dve.memset(tiny[:, 7:8], 0.0)

                dve.wait_ge(sc_copied, 8)
                chain(dve.tensor_copy(st.rearrange("p a b -> p (a b)"),
                                      s_all[:, bass.ds(r, 1), :].rearrange("p o n -> p (o n)")), True)
                for half in range(2):
                    d = dve.max(v16[:, half, 0:8], st[:, half, :])
                chain(d, True)
                for half in range(2):
                    dve.max_index(ix16[:, half, 0:8], v16[:, half, 0:8], st[:, half, :])
                    d = dve.match_replace(st2[:, half, :], v16[:, half, 0:8], st[:, half, :], LOWEST)
                chain(d, True)
                for half in range(2):
                    d = dve.max(v16[:, half, 8:16], st2[:, half, :])
                chain(d, True)
                for half in range(2):
                    dve.max_index(ix16[:, half, 8:16], v16[:, half, 8:16], st2[:, half, :])
                chain(dve.tensor_tensor(cand, v16[:, 0, :].unsqueeze(2).to_broadcast([P, TOPK, TOPK]),
                                        v16[:, 1, None, :].to_broadcast([P, TOPK, TOPK]), ALU.add), True)
                flat = cand.rearrange("p a b -> p (a b)")
                chain(dve.max(top16[:, 0:8], flat), True)
                dve.max_index(pos16[:, 0, 0:8], top16[:, 0:8], flat)
                chain(dve.match_replace(cand2, top16[:, 0:8], flat, LOWEST), True)
                chain(dve.max(top16[:, 8:16], cand2), True)
                chain(dve.max_index(pos16[:, 0, 8:16], top16[:, 8:16], cand2))
                dve.tensor_scalar(pos16[:, 1, :], pos16[:, 0, :], 4, None, ALU.logical_shift_right)
                dve.tensor_copy(ix16f, ix16[:, :, :])
                dve.tensor_scalar(gates[:, bass.ds(r, 1), :].rearrange("p o n -> p (o n)"), top16, top16[:, 0:1],
                                  None, ALU.subtract)
                chain(dve.tensor_scalar(pos16[:, 2, :], pos16[:, 0, :], 15, None, ALU.bitwise_and))
                chain(dve.tensor_copy(pos_f, pos16[:, 1:3, :]))
                cols = iota[:, None, 0:TOPK].to_broadcast([P, TOPK, TOPK])
                for which, pick in enumerate((pick_a, pick_b)):
                    d = dve.tensor_tensor(pick, pos_f[:, which, :].unsqueeze(2).to_broadcast([P, TOPK, TOPK]),
                                          cols, ALU.is_equal)
                chain(d)
                for which, pick in enumerate((pick_a, pick_b)):
                    d = dve.tensor_tensor(pick, pick, ix16f[:, which, None, :].to_broadcast([P, TOPK, TOPK]),
                                          ALU.mult)
                chain(d)
                for pick, dst in ((pick_a, idx1), (pick_b, idx2)):
                    d = dve.tensor_reduce(dst[:, bass.ds(r, 1), :].rearrange("p o n -> p (o n)"), pick, AXX,
                                          ALU.add)
                chain(d)
                assert step[0] == CHAIN_STEPS
            count[0] = base + 2 * PEER_HEADS * CHAIN_STEPS
            dve.wait_ge(vec, count[0])
            dve.memset(tiny[:, 6:7], 0.0).then_inc(gate_in, 1)
            dve.wait_ge(gate_exp, 1)
            link(dve.tensor_reduce(gate_sum, gates, AXX, ALU.add))
            link(dve.reciprocal(gate_sum, gate_sum))
            dve.tensor_tensor(gates, gates, gate_sum.unsqueeze(2).to_broadcast([P, 16, TOPK]), ALU.mult)\
                .then_inc(sel_ready, 1)
            dve.wait_ge(selT_ready, 1)
            link(dve.tensor_copy(sel_T[:, 0:2, :], ps[:, 2, :].rearrange("p (a b) -> p a b", a=2)))
            dve.tensor_copy(sel_T[:, 2, :], ps[:, 3, 0:T]).then_inc(selT_copied, 1)
            dve.wait_ge(selT_copied, 1)

            def one_hots(i, j):
                if i is not None:
                    dve.wait_ge(oh_used, at(i, 4, j - 3))
                for which, rows in enumerate((oh1, oh2)):
                    d = dve.tensor_tensor(rows[j], iota[:, None, :].to_broadcast([P, 4, P]),
                                          sel_T[:, which, bass.ds(at(i, 16, 4 * j), 4)].unsqueeze(2)
                                          .to_broadcast([P, 4, P]), ALU.is_equal)
                d.then_inc(oh_ready, 1)

            def meet_early(i, j):
                dve.wait_ge(w_evac, at(i, 4, j + 1))
                dst = routed_by_token[:, bass.ds(at(i, 16, 4 * j), 4), 0:EARLY]
                dve.tensor_tensor(dst, dst, ps[:, 2 + j % 4, :].rearrange("p (a b) -> p a b", a=4)[:, :, 0:EARLY],
                                  ALU.mult).then_inc(w_early, 1)

            dve.wait_ge(gemm_evac, PH_GATE.block)
            for j in range(4):
                one_hots(None, j)
                if j >= 2:
                    meet_early(None, j - 2)
            with dve.Fori(1, T // 16) as i:
                for j in range(4):
                    one_hots(i, j)
                    meet_early(i, j - 2)
            meet_early(None, T // 4 - 2)
            meet_early(None, T // 4 - 1)

            def route(b0, i, per):
                dve.wait_ge(gemm_evac, at(i, per, b0 + 1))
                b = b0 - B_UP
                dst = routed_v[:, b, :] if i is None else \
                    routed_v[:, bass.ds(i * per + b, 1), :].rearrange("p o t -> p (o t)")
                dve.tensor_tensor(dst, dst, gel[:, b0 % 2, :], ALU.mult).then_inc(routed, 1)

            def up_body(ph, i, first=False):
                for j, kind in enumerate(ph.pattern):
                    if kind == "a":
                        ada_step(ph, j, i, acc_last)
                    if kind == "w":
                        lo(ph, j, i)
                        if ph.nth(j) % 2 and not (first and ph.nth(j) == 1):
                            route(ph.block + ph.nth(j) // 2 - 1, i, ph.s_per // 2)

            dve.wait_ge(oh_used, T // 4)
            up_body(PH_GATE, None, True)
            with dve.Fori(1, PH_GATE.n) as i:
                up_body(PH_GATE, i)
            with dve.Fori(0, PH_UP.n) as i:
                up_body(PH_UP, i)
            mod_add(5, 6, mod_sum, 6)
            dve.tensor_tensor(mod[:, 5, :], mod[:, 5, :], gv[:, 3, :], ALU.mult).then_inc(mod_ready, 1)
            route(B_END - 1, None, 1)

            def down(i):
                for j in range(4):
                    if j % 2 == 0:
                        src = routed_v[:, j // 2, :] if i is None else \
                            routed_v[:, bass.ds(i * 2 + j // 2, 1), :].rearrange("p o t -> p (o t)")
                        dve.wait_ge(at_hi, at(i, 2, j // 2 + 1))
                        dve.tensor_tensor(a_lo[:, j // 2, :], src, a_hi[:, j // 2, :].bitcast(F32), ALU.subtract)\
                            .then_inc(at_lo, 1)
                    lo(PH_DOWN, j, i)

            dve.wait_ge(routed, EXPERT_BLOCKS - EARLY)
            down(None)
            with dve.Fori(1, PH_DOWN.n) as i:
                down(i)
            dve.wait_ge(split_used, PH_DOWN.s_end)
            for n in range(8):
                dve.tensor_copy(mixT[:, 2 * n:2 * n + 2, :], ps[:, n, :].rearrange("p (a b) -> p a b", a=2))\
                    .then_inc(ff_copied, 1)
            dve.wait_ge(ss_ready, 6)
            inverse_variance(ps[:, 7, 0:T], D, rs, var_ready)
            dve.wait_ge(rs_ready, 4)
            dve.wait_ge(x2_back, 16)
            for q in range(4):
                for kc in range(4 * q, 4 * q + 4):
                    d = dve.scalar_tensor_tensor(mixT[:, kc, :], mixT[:, kc, :], mod[:, 5, kc:kc + 1], rs,
                                                 ALU.mult, ALU.mult)
                link(d)
                s = slice(4 * q, 4 * q + 4)
                dve.tensor_tensor(mixT[:, s, :], mixT[:, s, :], xT[:, s, :], ALU.add).then_inc(out_ready, 1)


CHAIN_STEPS = 14


def kernel(x, c, w_ada, b_ada, g_pre_mix, g_post_mix, g_pre_ffn, g_post_ffn, w_in, lambda_q1, lambda_k1,
           lambda_q2, lambda_k2, g_subln, conv_w, conv_b, conv_ln_g, conv_ln_b, w_out, peer_wq, peer_k1,
           peer_k2, peer_u, peer_v):
    import numpy as np
    import concourse.bacc as bacc
    from concourse.bass_utils import run_bass_kernel_spmd

    def columns(v):
        return np.asarray(v).reshape(-1, P).T

    def blocks(w):
        w = np.asarray(w)
        return np.ascontiguousarray(w.reshape(KC, P, -1, P).transpose(2, 1, 0, 3)).reshape(-1, P, D)

    w_in_b = blocks(w_in[0])
    pairs = np.stack([w_in_b[24:32], w_in_b[32:40]], axis=1).reshape(BLOCKS, P, D)
    w_in_b = np.concatenate([pairs, w_in_b[0:24]])
    u = np.asarray(peer_u[0]).reshape(KEYS, KEYS, KC, P).transpose(0, 3, 2, 1)
    arrays = {
        "x": np.ascontiguousarray(np.asarray(x)[0].T.reshape(KC, P, T).transpose(1, 0, 2)).reshape(P, KC * T),
        "c": np.ascontiguousarray(columns(c)),
        "w_ada": np.asarray(w_ada)[0],
        "b_ada": np.ascontiguousarray(columns(b_ada)),
        "g_vecs": np.ascontiguousarray(np.stack([columns(g) for g in (g_pre_mix, g_post_mix, g_pre_ffn,
                                                                      g_post_ffn)], axis=1)),
        "w_in": w_in_b,
        "lambdas": np.stack([np.asarray(v)[0] for v in (lambda_q1, lambda_k1, lambda_q2, lambda_k2)]),
        "g_subln": np.ascontiguousarray(columns(g_subln)),
        "conv_w": np.ascontiguousarray(np.asarray(conv_w)[0].T.reshape(CONV_CHUNKS, P, TAPS).transpose(1, 0, 2)),
        "conv_vecs": np.ascontiguousarray(np.stack([columns(v) for v in (conv_b, conv_ln_g, conv_ln_b)], axis=1)),
        "w_out": blocks(np.concatenate([np.asarray(w_out)[0, D // 2:], np.asarray(w_out)[0, :D // 2]])),
        "peer_wq": blocks(peer_wq[0]),
        "peer_keys": np.stack([np.asarray(k)[0].T for k in (peer_k1, peer_k2)]),
        "peer_u": np.ascontiguousarray(u).reshape(KEYS, P, D),
        "peer_v": np.asarray(peer_v)[0].reshape(KEYS, P, D),
    }
    nc = bacc.Bacc("TRN2", target_bir_lowering=False, num_devices=1)
    aps = {n: nc.dram_tensor("in_" + n, a.shape, mybir.dt.from_np(a.dtype), kind="ExternalInput").ap()
           for n, a in arrays.items()}
    out = nc.dram_tensor("out_0", (P, KC * T), F32, kind="ExternalOutput").ap()
    build_block(nc, out=out, **aps)
    got = run_bass_kernel_spmd(nc, [{"in_" + n: a for n, a in arrays.items()}], core_ids=[0])
    y = got.results[0]["out_0"].reshape(P, KC, T).transpose(2, 1, 0).reshape(1, T, D)
    return np.ascontiguousarray(y)
```

```python
from contextlib import ExitStack
import math

import concourse.bass as bass
from concourse import mybir

P = 128
D = 2048
T = 256
KC = D // P
HEADS = 8
HEAD_DIM = 64
TAPS = 31
PAD = TAPS - 1
CONV_CHUNKS = 8
PEER_HEADS = 8
KEYS = 128
TOPK = 16
EPS = 1e-6
LAMBDA_INIT = 0.8 - 0.6 * math.exp(-0.3 * 0)
SCALE = 1.0 / math.sqrt(HEAD_DIM)
SLOPES = [2.0 ** (-8.0 * (h + 1.0) / HEADS) for h in range(HEADS)]
FAR = 1e30
LOWEST = -3e38

RAW = 4
WIDE = 8
UNIT = 1024
UCH = UNIT // P
IN_BLOCKS = 40
BLOCKS = D // P
EXPERT_BLOCKS = KEYS

EARLY = 2 * 2 * PEER_HEADS


def at(i, step, first):
    return first if i is None else i * step + first


STEPS = {"w": 1, "p": 2, "a": 1, "g": 1}


class Phase:

    def __init__(self, before, n, pattern, group=None, row=0, ring=RAW):
        assert len(pattern) % ring == 0
        self.ring, self.before = ring, before
        self.landings = before.landings_end if before else [0] * WIDE
        self.landings_end = [k + (n * len(pattern) // ring if place < ring else 0)
                             for place, k in enumerate(self.landings)]
        self.n, self.pattern, self.group, self.row = n, pattern, group, row
        self.u = before.u_end if before else 0
        self.first = {k: before.end[k] if before else 0 for k in STEPS}
        self.per = len(pattern)
        self.each = {k: pattern.count(k) for k in STEPS}
        self.u_end = self.u + n * self.per
        self.end = {k: self.first[k] + n * self.each[k] for k in STEPS}
        self.s, self.s_per, self.s_end = (x["w"] + x["p"] for x in (self.first, self.each, self.end))
        self.block = self.s // 2

    def nth(self, j):
        same = "ag" if self.pattern[j] in "ag" else "wp"
        return sum(k in same for k in self.pattern[:j])

    def landed(self, j, i):
        return at(i, 16 * (self.per // self.ring), 16 * (self.landings[j % self.ring] + j // self.ring + 1))

    def user_before(self, j):
        if j >= self.ring:
            return self, 0, j - self.ring
        ph = self.before
        while ph and j >= ph.ring:
            ph = ph.before
        return ph and (ph, ph.n - 1, ph.per - ph.ring + j)

    def halves(self, n):
        places = [j for j, k in enumerate(self.pattern) if k in "wp"]
        return places[2 * n:2 * n + 2]

    def done(self, j, i):
        kind = self.pattern[j]
        n = STEPS[kind]
        return at(i, n * self.each[kind], n * (self.first[kind] + self.pattern[:j].count(kind) + 1))


PH_SHIFT = Phase(None, KC // 4, "aaaaaaaa", 0, ring=WIDE)
PH_SCALE = Phase(PH_SHIFT, KC // 4, "aaaaaaaa", 1, ring=WIDE)
PH_GLU = Phase(PH_SCALE, BLOCKS // 4, "ppaappaa", 2, ring=WIDE)
PH_CONV = Phase(PH_GLU, BLOCKS // 4, "ppaappaa", 2, PH_GLU.n * 2, WIDE)
PH_QKV = Phase(PH_CONV, (IN_BLOCKS - BLOCKS) // 6, 2 * "ppappapp", 3, ring=WIDE)
PH_ATT = Phase(PH_QKV, (KC - 2 * PH_QKV.n) // 2, "gggg", 3, PH_QKV.n * 2)
PH_OUT = Phase(PH_ATT, BLOCKS // 2, "wwaawwaa", 4)
PH_WQ = Phase(PH_OUT, BLOCKS // 4, "wwwwwwww")
PH_EARLY = Phase(PH_WQ, EARLY // 2, "pppp")
PH_GATE = Phase(PH_EARLY, KC // 2, "wwawwawwawwa", 5)
PH_UP = Phase(PH_GATE, (EXPERT_BLOCKS - EARLY) // 4 - PH_GATE.n, "wwwwwwww")
PH_DOWN = Phase(PH_UP, EXPERT_BLOCKS // 4, "wwwwwwww")
ATT_UNITS = (0, 3, 6, 7, 9, 12, 14, 16, 16)
B_UP = PH_EARLY.block
B_END = B_UP + EXPERT_BLOCKS

F32 = mybir.dt.float32
F32R = mybir.dt.float32r
U32 = mybir.dt.uint32
ALU = mybir.AluOpType
ACT = mybir.ActivationFunctionType
AXX = mybir.AxisListType.X


def build_block(nc, x, c, w_ada, b_ada, g_vecs, w_in, lambdas, g_subln, conv_w, conv_vecs,
                w_out, peer_wq, peer_keys, peer_u, peer_v, out):
    with ExitStack() as ctx:
        def sb(name, shape, dt=F32):
            return ctx.enter_context(nc.sbuf_tensor(name, shape, dt))

        def sem(name):
            return ctx.enter_context(nc.semaphore(name))

        big = sb("big", [P, KEYS * T])
        routed_v = big[:, :].rearrange("p (i t) -> p i t", t=T)
        routed_by_token = big[:, :].rearrange("p (i t) -> p t i", t=T)

        def region(start, *shape):
            n = int(math.prod(shape))
            v = big[:, start:start + n]
            if len(shape) == 2:
                v = v.rearrange("p (a b) -> p a b", b=shape[1])
            if len(shape) == 3:
                v = v.rearrange("p (a b c) -> p a b c", b=shape[1], c=shape[2])
            return v

        xT = region(0, KC, T)
        hT = region(4096, KC, T)
        proj = region(8192, IN_BLOCKS, T)
        convT = region(8192, CONV_CHUNKS, T)
        conv_sq = region(10240, CONV_CHUNKS, T)
        mixT = region(8192, KC, T)
        squares = region(12288, KC, T)
        acc_even = region(18432, D)
        acc_odd = region(6144, D)
        head_row = region(20480, HEADS, P)
        head_col = region(21504, HEADS, HEADS)
        upad = region(22528, CONV_CHUNKS, T + PAD)
        oT = region(24832, HEADS, T)
        v_tok = region(26880, 2 * HEADS, P)
        probs = region(28928, 2, 2, 384)
        aT = region(30464, 2, 384)
        distm = region(31232, 384)
        conv_wt = region(31616, CONV_CHUNKS, TAPS)
        conv_v = region(31864, 3, CONV_CHUNKS)
        lam_in = region(31888, 4, HEAD_DIM)
        stat = region(32144, 2, T)
        keysT = region(16384, 2, KEYS)
        rs = region(16640, T)
        o_sq = region(4096, HEADS, T)
        o_rs = region(31888, T)
        s_all = region(12288, 16, 2 * KEYS)
        rt = 22528
        h_full = squares
        st = region(rt, 2, KEYS)
        st2 = region(rt + 256, 2, KEYS)
        cand = region(rt + 512, TOPK, TOPK)
        cand2 = region(rt + 768, TOPK * TOPK)
        pick_a = region(rt + 1024, TOPK, TOPK)
        pick_b = region(rt + 1280, TOPK, TOPK)
        v16 = region(rt + 1536, 2, TOPK)
        top16 = region(rt + 1568, TOPK)
        ix16f = region(rt + 1584, 2, TOPK)
        pos_f = region(rt + 1616, 2, TOPK)
        gates = region(rt + 1664, 16, TOPK)
        gate_sum = region(rt + 1920, 16)
        idx1 = region(rt + 2048, 16, TOPK)
        idx2 = region(rt + 2304, 16, TOPK)
        ix16 = sb("ix16", [P, 2, TOPK], U32)
        pos16 = sb("pos16", [P, 3, TOPK], U32)

        a_hi = sb("a_hi", [P, KC, T], F32R)
        a_lo = sb("a_lo", [P, KC, T], F32R)
        raw = sb("raw", [P, RAW, UNIT])
        ring = [raw[:, n, :] for n in range(RAW)] + \
            [region(26880 + n * UNIT, UNIT) for n in range(WIDE - RAW)]
        w_hi = sb("w_hi", [P, 2, UNIT], F32R)
        w_lo = sb("w_lo", [P, 2, UNIT], F32R)

        ones = sb("ones", [P, P])
        ident = sb("ident", [P, P])
        iota = sb("iota", [P, P])
        cT = sb("cT", [P, KC])
        mod_b = sb("mod_b", [P, 6 * KC])
        mod = sb("mod", [P, 6, KC])
        gv = sb("gv", [P, 4, KC])
        gsub = sb("gsub", [P, 1])
        scratch = sb("scratch", [P, 9 * T])
        sel_T = scratch[:, 0:3 * T].rearrange("p (a b) -> p a b", b=T)
        acc_last = scratch[:, 0:D]
        gel = sb("gel", [P, 2, T])

        def four_rows(v):
            return v.rearrange("p (t k) -> p t k", k=P)

        oh1 = (four_rows(raw[:, 2, 0:512]), four_rows(raw[:, 3, 0:512]), four_rows(scratch[:, 768:1280]),
               four_rows(scratch[:, 1792:2304]))
        oh2 = (four_rows(raw[:, 2, 512:1024]), four_rows(raw[:, 3, 512:1024]), four_rows(scratch[:, 1280:1792]),
               four_rows(gel[:, :, :].rearrange("p a b -> p (a b)")))
        early_w = sb("early_w", [P, 2, 4, EARLY])
        tiny = sb("tiny", [P, 32])
        lam_sum, lam_exp, neg_lam = tiny[:, 0:2], tiny[:, 2:4], tiny[:, 4:5]
        mx = [tiny[:, 8:12], tiny[:, 12:16]]
        sums = [tiny[:, 16:20], tiny[:, 20:24]]
        rcp = [tiny[:, 24:28], tiny[:, 28:32]]

        ps = ctx.enter_context(nc.psum_tensor("ps", [P, 8, 512], F32))
        x_saved = nc.dram_tensor("x_saved", (P, KC * T), F32, kind="Internal").ap()

        landed = [sem(f"landed{j}") for j in range(WIDE)]
        unit_scaled = sem("unit_scaled")
        c_in, x_in, small_in = sem("c_in"), sem("x_in"), sem("small_in")
        hi_ready, lo_ready, split_used, ada_used = (sem("hi_ready"), sem("lo_ready"), sem("split_used"),
                                                    sem("ada_used"))
        lo_pool, ada_pool = sem("lo_pool"), sem("ada_pool")
        unit_done = {"w": lo_ready, "p": lo_pool, "a": ada_used, "g": ada_pool}
        gemm_evac = sem("gemm_evac")
        consts, pool = sem("consts"), sem("pool")
        vec, s_first = sem("vec"), sem("s_first")
        sq_ready, ss_ready, var_ready, rs_ready = (sem("sq_ready"), sem("ss_ready"), sem("var_ready"),
                                                   sem("rs_ready"))
        silu_c, mod_sum, mod_ready = sem("silu_c"), sem("mod_sum"), sem("mod_ready")
        t_ready, h_hi, h_made, h_ready = sem("t_ready"), sem("h_hi"), sem("h_made"), sem("h_ready")
        glu_ready, tap = sem("glu_ready"), sem("tap")
        s_ready, s_read, neg_max, exp_done = sem("s_ready"), sem("s_read"), sem("neg_max"), sem("exp_done")
        a_ready, aT_ready, aT_copied = sem("a_ready"), sem("aT_ready"), sem("aT_copied")
        o_ready, o_copied, vt_ready, vt_copied = sem("o_ready"), sem("o_copied"), sem("vt_ready"), sem("vt_copied")
        lam_dots, lam_e = sem("lam_dots"), sem("lam_e")
        conv_stat = sem("conv_stat")
        conv_sq_ready, z_ready, y_ready = sem("conv_sq_ready"), sem("z_ready"), sem("y_ready")
        o_sq_ready, o_ss, o_var = sem("o_sq_ready"), sem("o_ss"), sem("o_var")
        o_root, o_spread = sem("o_root"), sem("o_spread")
        conv_var, conv_rs, conv_n = sem("conv_var"), sem("conv_rs"), sem("conv_n")
        x2_pool, out_pool = sem("x2_pool"), sem("out_pool")
        x2_ready, x2_saved, x2_back = sem("x2_ready"), sem("x2_saved"), sem("x2_back")
        sc_ready, sc_copied = sem("sc_ready"), sem("sc_copied")
        gate_in, gate_exp, sel_ready, selT_ready, selT_copied = (sem("gate_in"), sem("gate_exp"),
                                                                 sem("sel_ready"), sem("selT_ready"),
                                                                 sem("selT_copied"))
        oh_ready, gated_act, gated_pool, oh_used = (sem("oh_ready"), sem("gated_act"), sem("gated_pool"),
                                                    sem("oh_used"))
        w_evac, w_early, routed = sem("w_evac"), sem("w_early"), sem("routed")
        at_hi, at_lo, ff_copied, out_ready, out_done = (sem("at_hi"), sem("at_lo"), sem("ff_copied"),
                                                        sem("out_ready"), sem("out_done"))

        ada = w_ada.rearrange("(k p) n -> k p n", p=P)
        N_SMALL = 6
        block = ctx.enter_context(nc.Block())

        def low_part(engine, ph, j, i):
            s = ph.s + ph.nth(j)
            engine.wait_ge(hi_ready, at(i, ph.s_per, s + 1))
            steps = STEPS[ph.pattern[j]]
            for n in range(steps):
                part = slice(n * UNIT // steps, (n + 1) * UNIT // steps)
                engine.tensor_tensor(w_lo[:, s % 2, part], ring[j % ph.ring][:, part],
                                     w_hi[:, s % 2, part].bitcast(F32), ALU.subtract)\
                    .then_inc(unit_done[ph.pattern[j]], 1)

        @block.sync
        def _(sp):
            def slot_free(ph, j, i):
                if i is None:
                    if not ph.user_before(j):
                        return
                    before, it, place = ph.user_before(j)
                    count = before.done(place, it)
                elif j >= ph.ring:
                    before, place, count = ph, j - ph.ring, ph.done(j - ph.ring, i)
                else:
                    before, place = ph, j - ph.ring + ph.per
                    steps = STEPS[ph.pattern[place]] * ph.each[ph.pattern[place]]
                    count = at(i, steps, ph.done(place, None) - steps)
                sp.wait_ge(unit_done[before.pattern[place]], count)

            def bring(ph, i, w, block0=0):
                for j, kind in enumerate(ph.pattern):
                    nth = ph.nth(j)
                    slot_free(ph, j, i)
                    per, src = (ph.each[kind], ada) if kind in "ag" else (ph.s_per, w)
                    half = slice((nth % 2) * UNIT, (nth % 2 + 1) * UNIT)
                    if kind in "ag":
                        half = slice(ph.group * D + half.start, ph.group * D + half.stop)
                    row = nth // 2 + (ph.row if kind in "ag" else block0)
                    if i is None:
                        src = src[row, :, half]
                    else:
                        src = src[bass.ds(i * (per // 2) + row, 1), :, half].rearrange("o p n -> (o p) n")
                    if ph is PH_GATE and i is None and j in (2, 3):
                        sp.wait_ge(oh_used, T // 4)
                    sp.dma_start(ring[j % ph.ring], src).then_inc(landed[j % ph.ring], 16)

            for ph, w, block0 in ((PH_SHIFT, None, 0), (PH_SCALE, None, 0), (PH_GLU, w_in, 0),
                                  (PH_CONV, w_in, PH_CONV.block), (PH_QKV, w_in, BLOCKS),
                                  (PH_ATT, None, 0), (PH_OUT, w_out, 0),
                                  (PH_WQ, peer_wq, 0), (PH_EARLY, peer_u, 0), (PH_GATE, peer_u, EARLY),
                                  (PH_UP, peer_u, EARLY + 4 * PH_GATE.n), (PH_DOWN, peer_v, 0)):
                bring(ph, None, w, block0)
                with sp.Fori(1, ph.n) as i:
                    bring(ph, i, w, block0)
            sp.wait_ge(at_lo, EXPERT_BLOCKS)
            sp.dma_start(xT.rearrange("p a b -> p (a b)"), x_saved).then_inc(x2_back, 16)
            for q in range(4):
                if q < 3:
                    sp.wait_ge(out_ready, q + 1)
                else:
                    sp.wait_ge(out_pool, 1)
                sp.dma_start(out[:, q * 1024:(q + 1) * 1024],
                             mixT[:, 4 * q:4 * q + 4, :].rearrange("p a b -> p (a b)")).then_inc(out_done, 16)
            sp.wait_ge(out_done, 64)

        @block.gpsimd
        def _(gp):
            gp.memset(ones[:, :], 1.0).then_inc(consts, 1)
            gp.memset(ident[:, :], 0.0).then_inc(pool, 1)
            gp.wait_ge(pool, 1)
            gp.affine_select(out=ident[:, :], in_=ident[:, :], compare_op=ALU.not_equal, fill=1.0, base=0,
                             pattern=[[-1, P]], channel_multiplier=1).then_inc(consts, 1)
            gp.iota(iota[:, :], pattern=[[1, P]], base=0, channel_multiplier=0,
                    allow_small_or_imprecise_dtypes=True).then_inc(consts, 1)
            gp.iota(distm[:, 0:128], pattern=[[-1, 128]], base=0, channel_multiplier=1,
                    allow_small_or_imprecise_dtypes=True).then_inc(pool, 1)
            gp.iota(distm[:, 128:384], pattern=[[-1, 256]], base=128, channel_multiplier=1,
                    allow_small_or_imprecise_dtypes=True).then_inc(pool, 1)
            gp.wait_ge(pool, 3)
            gp.affine_select(out=distm[:, 0:128], in_=distm[:, 0:128], compare_op=ALU.is_ge, fill=FAR, base=0,
                             pattern=[[-1, 128]], channel_multiplier=1).then_inc(consts, 1)
            gp.affine_select(out=distm[:, 128:384], in_=distm[:, 128:384], compare_op=ALU.is_ge, fill=FAR,
                             base=128, pattern=[[-1, 256]], channel_multiplier=1).then_inc(consts, 1)
            gp.memset(head_row, 0.0).then_inc(pool, 1)
            gp.memset(head_col, 0.0).then_inc(pool, 1)
            gp.wait_ge(pool, 5)
            gp.affine_select(out=head_row, in_=head_row, compare_op=ALU.not_equal, fill=1.0, base=0,
                             pattern=[[-1, HEADS], [0, P]], channel_multiplier=1).then_inc(consts, 1)
            gp.affine_select(out=head_col, in_=head_col, compare_op=ALU.not_equal, fill=1.0, base=0,
                             pattern=[[1, HEADS], [-1, HEADS]], channel_multiplier=0).then_inc(consts, 1)
            gp.memset(upad[:, :, 0:PAD], 0.0).then_inc(consts, 1)

            def low_parts(ph, start=0):
                with gp.Fori(start, ph.n) as i:
                    for j, kind in enumerate(ph.pattern):
                        if kind == "p":
                            low_part(gp, ph, j, i)

            def last_quarter(dst, norm, done):
                last = slice(KC - 4, KC)
                gp.wait_ge(rs_ready, norm)
                gp.tensor_tensor(mixT[:, last, :], mixT[:, last, :], rs[:, None, :].to_broadcast([P, 4, T]),
                                 ALU.mult).then_inc(pool, 1)
                gp.wait_ge(pool, 6 if norm == 2 else 7)
                gp.tensor_tensor(dst[:, last, :], mixT[:, last, :], xT[:, last, :], ALU.add).then_inc(done, 1)

            def low_of_activations(n_made, n_hi):
                for kc in range(KC):
                    gp.wait_ge(h_made, n_made + kc + 1)
                    gp.wait_ge(h_hi, n_hi + kc + 1)
                    gp.tensor_tensor(a_lo[:, kc, :], h_full[:, kc, :], a_hi[:, kc, :].bitcast(F32), ALU.subtract)\
                        .then_inc(h_ready, 1)

            for j in range(2):
                low_part(gp, PH_GLU, j, None)
            low_of_activations(0, 0)
            for j in range(2, PH_GLU.per):
                if PH_GLU.pattern[j] == "p":
                    low_part(gp, PH_GLU, j, None)
            low_parts(PH_GLU, 1)
            low_parts(PH_CONV)
            low_parts(PH_QKV)
            for k in range(PH_ATT.n * PH_ATT.per):
                half = slice((k % 2) * UNIT, (k % 2 + 1) * UNIT)
                gp.wait_ge(unit_scaled, k + 1)
                if k >= 2:
                    gp.wait_ge(ada_pool, k - 1)
                else:
                    gp.wait_ge(ada_used, PH_QKV.end["a"])
                gp.tensor_tensor(acc_odd[:, half], acc_odd[:, half], ring[k % PH_ATT.ring], ALU.add)\
                    .then_inc(ada_pool, 1)
            gp.wait_ge(gemm_evac, PH_WQ.block)
            last_quarter(xT, 2, x2_pool)
            low_of_activations(KC, KC + 8)
            low_parts(PH_EARLY)
            def gated(i, j):
                gp.wait_ge(oh_ready, at(i, 4, j + 1))
                gp.tensor_tensor(oh2[j][:, 1:4, :], oh2[j][:, 1:4, :],
                                 sel_T[:, 2, bass.ds(at(i, 16, 4 * j + 1), 3)].unsqueeze(2)
                                 .to_broadcast([P, 3, P]), ALU.mult).then_inc(gated_pool, 1)

            def meet_early(i, j):
                gp.wait_ge(w_evac, at(i, 4, j + 1))
                dst = routed_by_token[:, bass.ds(at(i, 16, 4 * j), 4), 0:EARLY]
                gp.tensor_tensor(dst, dst, early_w[:, j % 2], ALU.mult).then_inc(w_early, 1)

            gp.wait_ge(selT_copied, 1)
            for j in range(4):
                gated(None, j)
                if j >= 2:
                    meet_early(None, j - 2)
            with gp.Fori(1, T // 16) as i:
                for j in range(4):
                    gated(i, j)
                    meet_early(i, j - 2)
            meet_early(None, T // 4 - 2)
            meet_early(None, T // 4 - 1)
            gp.wait_ge(ff_copied, 8)
            gp.wait_ge(x2_back, 16)
            last_quarter(mixT, 4, out_pool)

        @block.scalar
        def _(act):
            act.dma_start(cT[:, :], c).then_inc(c_in, 16)
            act.dma_start(mod_b[:, :], b_ada).then_inc(small_in, 16)
            act.dma_start(gv[:, :, :], g_vecs).then_inc(small_in, 16)
            act.dma_start(gsub[:, :], g_subln).then_inc(small_in, 16)
            act.dma_start(conv_wt, conv_w).then_inc(small_in, 16)
            act.dma_start(conv_v, conv_vecs).then_inc(small_in, 16)
            act.dma_start(lam_in, lambdas.partition_broadcast(P)).then_inc(small_in, 16)
            act.dma_start(xT.rearrange("p a b -> p (a b)"), x).then_inc(x_in, 16)
            act.wait_ge(c_in, 16)
            act.activation(cT[:, :], cT[:, :], ACT.Silu).then_inc(silu_c, 1)
            act.wait_ge(x_in, 16)
            act.activation(squares, xT, ACT.Square).then_inc(sq_ready, 1)
            act.wait_ge(lam_dots, 2)
            act.activation(lam_exp, lam_sum, ACT.Exp).then_inc(lam_e, 1)

            def root(n):
                act.wait_ge(var_ready, n)
                act.activation(rs, rs, ACT.Sqrt).then_inc(rs_ready, 1)

            def modulated(shift, n):
                for kc in range(KC):
                    act.wait_ge(t_ready, n + kc + 1)
                    act.activation(a_hi[:, kc, :], hT[:, kc, :], ACT.Identity, bias=mod[:, shift, kc:kc + 1])\
                        .then_inc(h_hi, 1)

            def hi(ph, j, i):
                s = ph.s + ph.nth(j)
                act.wait_ge(landed[j % ph.ring], ph.landed(j, i))
                if s >= 2 or i is not None:
                    act.wait_ge(split_used, at(i, ph.s_per, s - 1))
                act.activation(w_hi[:, s % 2, :], ring[j % ph.ring], ACT.Copy).then_inc(hi_ready, 1)

            def chunk(buf, b0, i, per):
                if i is None:
                    return buf[:, b0, :]
                return buf[:, bass.ds(i * per + b0, 1), :].rearrange("p o t -> p (o t)")

            def whole(b0, i, per):
                act.wait_ge(split_used, at(i, 2 * per, 2 * b0 + 2))

            def evac(buf, first_block):
                def put(b0, i, per):
                    whole(b0, i, per)
                    act.activation(chunk(buf, b0 - first_block, i, per), ps[:, b0 % 2, 0:T], ACT.Copy)\
                        .then_inc(gemm_evac, 1)
                return put

            def split_and_put(ph, i, put, first=False, skip=0):
                for j, kind in enumerate(ph.pattern[skip:], skip):
                    if kind != "a":
                        hi(ph, j, i)
                        if ph.nth(j) % 2 and not (first and ph.nth(j) == 1):
                            put(ph.block + ph.nth(j) // 2 - 1, i, ph.s_per // 2)

            def run(ph, put, start=0, first=False):
                if first:
                    split_and_put(ph, None, put, True)
                    start = 1
                with act.Fori(start, ph.n) as i:
                    split_and_put(ph, i, put)

            to_proj = evac(proj, 0)

            def to_glu(b0, i, per):
                if b0 % 2 == 0:
                    to_proj(b0, i, per)
                    return
                whole(b0, i, per)
                act.activation(chunk(proj, b0, i, per), ps[:, b0 % 2, 0:T], ACT.Sigmoid).then_inc(gemm_evac, 1)

            root(1)
            for j in range(2):
                hi(PH_GLU, j, None)
            modulated(0, 0)
            split_and_put(PH_GLU, None, to_glu, skip=2)
            run(PH_GLU, to_glu, start=1)
            run(PH_CONV, to_glu)
            hi(PH_QKV, 0, None)
            hi(PH_QKV, 1, None)
            to_glu(BLOCKS - 1, None, 1)
            split_and_put(PH_QKV, None, to_proj, skip=2)
            run(PH_QKV, to_proj, start=1)
            to_proj(IN_BLOCKS - 1, None, 1)

            def exps(h):
                act.wait_ge(neg_max, h + 1)
                for m in range(2):
                    for qb, (a, b) in enumerate(((0, 128), (128, 384))):
                        done = act.activation(probs[:, h % 2, m, a:b], probs[:, h % 2, m, a:b], ACT.Exp,
                                              bias=mx[h % 2][:, 2 * m + qb:2 * m + qb + 1], scale=SCALE,
                                              accum_out=sums[h % 2][:, 2 * m + qb:2 * m + qb + 1])
                done.then_inc(exp_done, 1)

            exps(0)
            exps(1)
            for h in range(HEADS):
                act.wait_ge(aT_ready, h + 1)
                if h >= 2:
                    act.wait_ge(o_ready, h - 1)
                act.activation(aT[:, h % 2, :], ps[:, 0, 0:384], ACT.Copy).then_inc(aT_copied, 1)
                act.wait_ge(o_ready, h + 1)
                act.activation(oT[:, h, :], ps[:, 1, 0:T], ACT.Copy).then_inc(o_copied, 1)
                if h + 2 < HEADS:
                    exps(h + 2)
                for k in range(ATT_UNITS[h], ATT_UNITS[h + 1]):
                    j, i = k % PH_ATT.per, k // PH_ATT.per
                    kc = PH_ATT.row + k // 2
                    act.wait_ge(landed[j % PH_ATT.ring], PH_ATT.landed(j, i))
                    act.activation(ring[j % PH_ATT.ring], ring[j % PH_ATT.ring], ACT.Copy, scale=cT[:, kc:kc + 1])\
                        .then_inc(unit_scaled, 1)
                if h == 2:
                    act.wait_ge(conv_stat, 1)
                    act.activation(conv_sq, convT, ACT.Square).then_inc(conv_sq_ready, 1)
                act.wait_ge(o_copied, h + 1)
                act.activation(o_sq[:, h, :], oT[:, h, :], ACT.Square).then_inc(o_sq_ready, 1)
                if h == 5:
                    act.wait_ge(conv_var, 1)
                    act.activation(stat[:, 1, :], stat[:, 1, :], ACT.Sqrt).then_inc(conv_rs, 1)
                if h == 6:
                    act.wait_ge(conv_n, 1)
                    for ch in range(CONV_CHUNKS):
                        act.activation(convT[:, ch, :], convT[:, ch, :], ACT.Silu, bias=conv_v[:, 2, ch:ch + 1],
                                       scale=conv_v[:, 1, ch:ch + 1]).then_inc(z_ready, 1)
            for n in range(4):
                act.wait_ge(z_ready, 2 * n + 2)
                act.activation(a_hi[:, 2 * n:2 * n + 2, :], convT[:, 2 * n:2 * n + 2, :], ACT.Copy).then_inc(h_hi, 1)
            act.wait_ge(o_var, 1)
            act.activation(o_rs[0:HEADS, :], o_rs[0:HEADS, :], ACT.Sqrt).then_inc(o_root, 1)
            for j in range(2):
                hi(PH_OUT, j, None)
            for n in range(4):
                act.wait_ge(y_ready, n + 1)
                act.activation(a_hi[:, 8 + 2 * n:10 + 2 * n, :], oT[:, 2 * n:2 * n + 2, :], ACT.Copy)\
                    .then_inc(h_hi, 1)
            act.dma_start(keysT[:, 0, :], peer_keys[0]).then_inc(small_in, 16)
            act.dma_start(keysT[:, 1, :], peer_keys[1]).then_inc(small_in, 16)

            def mix_out(b0, i, per):
                whole(b0, i, per)
                b = b0 - PH_OUT.block
                gate = mod[:, 2, bass.ds(at(i, per, b), 1)]
                act.activation(chunk(mixT, b, i, per), ps[:, b0 % 2, 0:T], ACT.Copy, scale=gate)\
                    .then_inc(gemm_evac, 1)
                act.activation(chunk(squares, b, i, per), ps[:, b0 % 2, 0:T], ACT.Square).then_inc(sq_ready, 1)

            act.wait_ge(mod_ready, 2)
            act.wait_ge(h_ready, KC + 8)
            for j in range(2, PH_OUT.per):
                if PH_OUT.pattern[j] == "w":
                    hi(PH_OUT, j, None)
            mix_out(PH_OUT.block, None, 1)
            run(PH_OUT, mix_out, start=1)
            mix_out(PH_WQ.block - 1, None, 1)
            root(2)
            for q in (0, 1, 3, 2):
                if q < 3:
                    act.wait_ge(x2_ready, q + 1)
                else:
                    act.wait_ge(x2_pool, 1)
                act.activation(squares[:, 4 * q:4 * q + 4, :], xT[:, 4 * q:4 * q + 4, :], ACT.Square)\
                    .then_inc(sq_ready, 1)
            act.dma_start(x_saved, xT.rearrange("p a b -> p (a b)")).then_inc(x2_saved, 16)
            for j in range(2):
                hi(PH_WQ, j, None)
            root(3)
            modulated(3, KC)

            to_q = evac(mixT, PH_WQ.block)
            split_and_put(PH_WQ, None, to_q, skip=2)
            run(PH_WQ, to_q, start=1)
            to_q(PH_EARLY.block - 1, None, 1)
            for j in range(2):
                hi(PH_EARLY, j, None)
            for n in range(8):
                act.wait_ge(sc_ready, n + 1)
                act.activation(s_all[:, 2 * n:2 * n + 2, :], ps[:, 2 + n % 2, :].rearrange("p (a b) -> p a b", a=2),
                               ACT.Copy).then_inc(sc_copied, 1)

            def gelu_stays(b0, i, per):
                whole(b0, i, per)
                act.activation(chunk(routed_v, b0 - B_UP, i, per), ps[:, b0 % 2, 0:T], ACT.Gelu)\
                    .then_inc(gemm_evac, 1)

            act.wait_ge(x2_saved, 16)
            split_and_put(PH_EARLY, None, gelu_stays, first=True, skip=2)
            run(PH_EARLY, gelu_stays, start=1)
            act.wait_ge(gate_in, 1)
            act.activation(gates, gates, ACT.Exp).then_inc(gate_exp, 1)
            gelu_stays(PH_GATE.block - 1, None, 1)
            for j in range(2):
                hi(PH_GATE, j, None)

            def gated(i, j):
                act.wait_ge(oh_ready, at(i, 4, j + 1))
                act.activation(oh2[j][:, 0, :], oh2[j][:, 0, :], ACT.Copy,
                               scale=sel_T[:, 2, bass.ds(at(i, 16, 4 * j), 1)]).then_inc(gated_act, 1)

            def put_weights(i, j):
                act.wait_ge(oh_used, at(i, 4, j + 1))
                bank = ps[:, 2 + j % 4, :].rearrange("p (a b) -> p a b", a=4)
                act.activation(routed_by_token[:, bass.ds(at(i, 16, 4 * j), 4), EARLY:], bank[:, :, EARLY:], ACT.Copy)
                if i is not None or j >= 2:
                    act.wait_ge(w_early, at(i, 4, j - 1))
                act.activation(early_w[:, j % 2], bank[:, :, 0:EARLY], ACT.Copy).then_inc(w_evac, 1)

            act.wait_ge(selT_copied, 1)
            for j in range(4):
                if j >= 2:
                    put_weights(None, j - 2)
                gated(None, j)
            with act.Fori(1, T // 16) as i:
                for j in range(4):
                    put_weights(i, j - 2)
                    gated(i, j)
            put_weights(None, T // 4 - 2)
            put_weights(None, T // 4 - 1)

            def gelu(b0, i, per):
                whole(b0, i, per)
                rel = b0 - PH_GATE.block
                if rel >= 2 or i is not None:
                    act.wait_ge(routed, at(i, per, rel - 1))
                act.activation(gel[:, b0 % 2, :], ps[:, b0 % 2, 0:T], ACT.Gelu).then_inc(gemm_evac, 1)

            act.wait_ge(w_early, T // 4)
            split_and_put(PH_GATE, None, gelu, first=True, skip=2)
            run(PH_GATE, gelu, start=1)
            run(PH_UP, gelu)
            gelu(B_END - 1, None, 1)

            def down(i):
                for j in range(PH_DOWN.per):
                    if j % 2 == 0:
                        if i is not None:
                            act.wait_ge(split_used, at(i, PH_DOWN.per, PH_DOWN.s + j + 2 - PH_DOWN.per))
                        act.activation(a_hi[:, j // 2, :], chunk(routed_v, j // 2, i, PH_DOWN.per // 2), ACT.Copy)\
                            .then_inc(at_hi, 1)
                    hi(PH_DOWN, j, i)

            act.wait_ge(split_used, PH_DOWN.s)
            down(None)
            act.wait_ge(routed, EXPERT_BLOCKS - EARLY)
            with act.Fori(1, PH_DOWN.n) as i:
                down(i)
            for n in range(8):
                act.wait_ge(ff_copied, n + 1)
                act.activation(squares[:, 2 * n:2 * n + 2, :].rearrange("p a b -> p (a b)"), ps[:, n, :], ACT.Square)\
                    .then_inc(sq_ready, 1)
            root(4)

        @block.tensor
        def _(pe):
            def sum_squares(counts, bank=7, order=(0, 1, 2, 3)):
                for n in range(KC):
                    kc = 4 * order[n // 4] + n % 4
                    pe.wait_ge(sq_ready, counts[kc])
                    done = pe.matmul(ps[:, bank, 0:T], ones[:, :], squares[:, kc, :], start=n == 0, stop=n == KC - 1)
                done.then_inc(ss_ready, 1)

            def modulation(group, units, used=ada_used):
                acc = (acc_even, acc_odd, acc_even, acc_odd, acc_even, acc_last)[group]
                for dc in range(KC):
                    if dc % UCH == 0:
                        pe.wait_ge(used, units - 1 + dc // UCH)
                    done = pe.matmul(ps[:, 6, group * KC + dc:group * KC + dc + 1], acc[:, dc * P:(dc + 1) * P],
                                     ones[:, 0:1], start=True, stop=True)
                done.then_inc(mod_sum, 1)

            def product(ph, n, i, chunks=None):
                b = ph.block + n
                if b >= 2 or i is not None:
                    pe.wait_ge(gemm_evac, at(i, ph.s_per // 2, b - 1))
                for half in range(2):
                    place = ph.halves(n)[half]
                    steps = STEPS[ph.pattern[place]]
                    for k in range(UCH):
                        kc = half * UCH + k
                        if k * steps % UCH == 0:
                            pe.wait_ge(unit_done[ph.pattern[place]],
                                       ph.done(place, i) - (steps - 1 - k * steps // UCH))
                        if chunks is not None:
                            pe.wait_ge(h_ready, chunks[kc])
                        for m, (w, a) in enumerate(((w_hi, a_hi), (w_hi, a_lo), (w_lo, a_hi))):
                            done = pe.matmul(ps[:, b % 2, 0:T], w[:, half, k * P:(k + 1) * P], a[:, kc, :],
                                             start=kc == 0 and m == 0, stop=kc == KC - 1 and m == 2)
                    done.then_inc(split_used, 1)

            def run(ph, chunks=None, after=None):
                if chunks:
                    for n in range(ph.s_per // 2):
                        product(ph, n, None, chunks if n == 0 else None)
                        if after:
                            after(n, None)
                with pe.Fori(1 if chunks else 0, ph.n) as i:
                    for n in range(ph.s_per // 2):
                        product(ph, n, i)
                        if after:
                            after(n, i)

            pe.wait_ge(consts, 8)
            sum_squares([1] * KC)
            modulation(0, PH_SHIFT.end["a"])
            modulation(1, PH_SCALE.end["a"])
            run(PH_GLU, chunks=[kc + 1 for kc in range(KC)])
            run(PH_CONV)
            run(PH_QKV)

            pe.wait_ge(gemm_evac, IN_BLOCKS)

            def scores(h):
                if h >= 2:
                    pe.wait_ge(s_read, h - 1)
                q, k = proj[:, 16 + h, :], proj[:, 24 + h, :]
                for m in range(2):
                    r = slice(64 * m, 64 * m + 64)
                    bank = 2 + 2 * (h % 2) + m
                    pe.matmul(ps[:, bank, 0:128], q[r, 0:128], k[r, 0:128], start=True, stop=True)
                    done = pe.matmul(ps[:, bank, 128:384], q[r, 128:256], k[r, :], start=True, stop=True)
                done.then_inc(s_ready, 1)

            scores(0)
            scores(1)
            for n in range(4):
                if n >= 2:
                    pe.wait_ge(vt_copied, n - 1)
                for j in range(4):
                    done = pe.transpose(ps[:, 7 * (n % 2), j * P:(j + 1) * P],
                                        proj[:, 32 + 2 * n + j // 2, (j % 2) * P:(j % 2 + 1) * P], ident[:, :])
                done.then_inc(vt_ready, 1)

            def over_channels(src, ready):
                pe.wait_ge(*ready)
                for ch in range(CONV_CHUNKS):
                    done = pe.matmul(ps[:, 7, 0:T], ones[:, :], src[:, ch, :], start=ch == 0,
                                     stop=ch == CONV_CHUNKS - 1)
                done.then_inc(ss_ready, 1)

            def head_squares(h):
                pe.wait_ge(o_sq_ready, h + 1)
                return pe.matmul(ps[0:HEADS, 7, 0:T], head_col[:, h, :], o_sq[:, h, :], start=h == 0,
                                 stop=h == HEADS - 1)

            for h in range(HEADS):
                if h + 2 < HEADS:
                    scores(h + 2)
                if h == 2:
                    modulation(2, PH_CONV.end["a"])
                pe.wait_ge(a_ready, h + 1)
                pe.wait_ge(vt_copied, 4)
                if h >= 1:
                    pe.wait_ge(aT_copied, h)
                for j in range(3):
                    done = pe.transpose(ps[:, 0, j * P:(j + 1) * P], probs[:, h % 2, 0, j * P:(j + 1) * P],
                                        ident[:, :])
                done.then_inc(aT_ready, 1)
                pe.wait_ge(aT_copied, h + 1)
                if h >= 1:
                    pe.wait_ge(o_copied, h)
                pe.matmul(ps[:, 1, 0:128], v_tok[:, 2 * h, :], aT[:, h % 2, 0:128], start=True, stop=True)
                pe.matmul(ps[:, 1, 128:256], v_tok[:, 2 * h, :], aT[:, h % 2, 128:256], start=True, stop=False)
                pe.matmul(ps[:, 1, 128:256], v_tok[:, 2 * h + 1, :], aT[:, h % 2, 256:384], start=False,
                          stop=True).then_inc(o_ready, 1)
                if h == 0:
                    over_channels(convT, (tap, TAPS * CONV_CHUNKS))
                if h == 3:
                    over_channels(conv_sq, (conv_sq_ready, 1))
                if h == 5:
                    pe.wait_ge(conv_var, 1)
                    for g in range(4):
                        head_squares(g)
                if h >= 5:
                    head_squares(h - 1)
            head_squares(HEADS - 1).then_inc(o_ss, 1)
            modulation(3, PH_ATT.end["g"], ada_pool)
            pe.wait_ge(o_root, 1)
            for h in range(HEADS):
                done = pe.matmul(ps[:, 2 + h // 2, (h % 2) * T:(h % 2 + 1) * T], head_row[0:HEADS, h, :],
                                 o_rs[0:HEADS, :], start=True, stop=True)
                if h % 2:
                    done.then_inc(o_spread, 1)

            def mix_sum(b, i):
                pe.wait_ge(sq_ready, at(i, 2, b + 2))
                src = squares[:, b, :] if i is None else \
                    squares[:, bass.ds(i * 2 + b, 1), :].rearrange("p o t -> p (o t)")
                return pe.matmul(ps[:, 7, 0:T], ones[:, :], src, start=i is None and b == 0, stop=False,
                                 skip_group_check=True)

            def behind(n, i):
                if n or i is not None:
                    mix_sum(n - 1, i)

            y_chunks = [KC + kc // 2 + 1 for kc in range(KC)]
            run(PH_OUT, chunks=y_chunks, after=behind)
            modulation(4, PH_OUT.end["a"])
            mix_sum(BLOCKS - 1, None).then_inc(ss_ready, 1)
            sum_squares([KC + 2 + (0, 1, 3, 2)[kc // 4] for kc in range(KC)], order=(0, 1, 3, 2))
            run(PH_WQ, chunks=[KC + 9 + kc for kc in range(KC)])

            pe.wait_ge(gemm_evac, B_UP)
            pe.wait_ge(small_in, 16 * (N_SMALL + 2))
            for n in range(8):
                if n >= 2:
                    pe.wait_ge(sc_copied, n - 1)
                for j in range(4):
                    r, half = 2 * n + j // 2, j % 2
                    tt, h = r // 8, r % 8
                    done = pe.matmul(ps[:, 2 + n % 2, j * KEYS:(j + 1) * KEYS],
                                     mixT[:, 2 * h + half, tt * P:(tt + 1) * P], keysT[:, half, :],
                                     start=True, stop=True)
                done.then_inc(sc_ready, 1)
            run(PH_EARLY)
            pe.wait_ge(sc_copied, 8)
            pe.wait_ge(sel_ready, 1)
            for n, src in enumerate((idx1, idx2, gates)):
                flat = src.rearrange("p r k -> p (r k)")
                for tt in range(2):
                    done = pe.transpose(ps[:, 2 + n // 2, (n % 2) * T + tt * P:(n % 2) * T + (tt + 1) * P],
                                        flat[:, tt * P:(tt + 1) * P], ident[:, :])
            done.then_inc(selT_ready, 1)

            def weights(i, j):
                pe.wait_ge(gated_act, at(i, 4, j + 1))
                pe.wait_ge(gated_pool, at(i, 4, j + 1))
                if i is not None:
                    pe.wait_ge(w_evac, at(i, 4, j - 3))
                for t in range(4):
                    done = pe.matmul(ps[:, 2 + j, t * P:(t + 1) * P], oh2[j][:, t, :], oh1[j][:, t, :],
                                     start=True, stop=True)
                done.then_inc(oh_used, 1)

            pe.wait_ge(selT_copied, 1)
            for j in range(4):
                weights(None, j)
            with pe.Fori(1, T // 16) as i:
                for j in range(4):
                    weights(i, j)

            run(PH_GATE)
            modulation(5, PH_GATE.end["a"])
            run(PH_UP)

            def down(i):
                for j in range(PH_DOWN.per):
                    blk = j // 2
                    if j % 2 == 0:
                        pe.wait_ge(at_lo, at(i, PH_DOWN.per // 2, blk + 1))
                    pe.wait_ge(lo_ready, PH_DOWN.done(j, i))
                    for k in range(UCH):
                        dt = (j % 2) * UCH + k
                        for n, (w, a) in enumerate(((w_hi, a_hi), (w_hi, a_lo), (w_lo, a_hi))):
                            done = pe.matmul(ps[:, dt // 2, (dt % 2) * T:(dt % 2 + 1) * T],
                                             w[:, j % 2, k * P:(k + 1) * P], a[:, blk, :],
                                             start=i is None and blk == 0 and n == 0 and dt % 2 == 0,
                                             stop=False, skip_group_check=True)
                    done.then_inc(split_used, 1)

            pe.wait_ge(gemm_evac, B_END)
            pe.wait_ge(mod_ready, 4)
            down(None)
            with pe.Fori(1, PH_DOWN.n) as i:
                down(i)
            sum_squares([KC + 6 + kc // 2 for kc in range(KC)], bank=0)

        @block.vector
        def _(dve):
            count = [0]

            def link(ins):
                count[0] += 1
                ins.then_inc(vec, 1)
                dve.wait_ge(vec, count[0])

            def bcast_t(v, n=KC):
                return v[:, None, :].to_broadcast([P, n, T])

            def inverse_variance(bank, n, dst, done):
                link(dve.tensor_scalar(dst, bank, 1.0 / n, EPS, ALU.mult, ALU.add))
                dve.reciprocal(dst, dst).then_inc(done, 1)

            dve.wait_ge(silu_c, 1)

            def ada_step(ph, j, i, acc):
                nth, unit = ph.nth(j), ring[j % ph.ring]
                dve.wait_ge(landed[j % ph.ring], ph.landed(j, i))
                dst = acc[:, (nth % 2) * UNIT:(nth % 2 + 1) * UNIT]
                if i is None and ph.row == 0 and nth < 2:
                    dve.tensor_scalar(dst, unit, cT[:, 0:1], None, ALU.mult).then_inc(ada_used, 1)
                    return
                dve.wait_ge(ada_used, at(i, ph.each["a"], ph.first["a"] + nth - 1))
                kc = at(i, ph.each["a"] // 2, ph.row + nth // 2)
                dve.scalar_tensor_tensor(dst, unit, cT[:, bass.ds(kc, 1)], dst, ALU.mult, ALU.add)\
                    .then_inc(ada_used, 1)

            def sums_of(ph, acc):
                for j in range(ph.per):
                    ada_step(ph, j, None, acc)
                with dve.Fori(1, ph.n) as i:
                    for j in range(ph.per):
                        ada_step(ph, j, i, acc)

            def lo(ph, j, i):
                low_part(dve, ph, j, i)

            def residual(dst, done):
                for q in range(3):
                    s = slice(4 * q, 4 * q + 4)
                    link(dve.tensor_tensor(mixT[:, s, :], mixT[:, s, :], bcast_t(rs, 4), ALU.mult))
                    dve.tensor_tensor(dst[:, s, :], mixT[:, s, :], xT[:, s, :], ALU.add).then_inc(done, 1)

            def mod_add(a, b, *ready):
                if ready:
                    dve.wait_ge(*ready)
                link(dve.tensor_tensor(mod[:, a:b, :], ps[:, 6, a * KC:b * KC].rearrange("p (a b) -> p a b", b=KC),
                                       mod_b[:, a * KC:b * KC].rearrange("p (a b) -> p a b", b=KC), ALU.add))

            def scaled(group, g):
                dve.scalar_tensor_tensor(mod[:, group, :], mod[:, group, :], 1.0, gv[:, g, :], ALU.add, ALU.mult)\
                    .then_inc(mod_ready, 1)

            def modulated(scale, shift, n):
                for kc in range(KC + 1):
                    if kc < KC:
                        dve.scalar_tensor_tensor(hT[:, kc, :], xT[:, kc, :], mod[:, scale, kc:kc + 1], rs, ALU.mult,
                                                 ALU.mult).then_inc(t_ready, 1)
                    if kc >= 1:
                        dve.wait_ge(t_ready, n + kc)
                        dve.tensor_scalar(h_full[:, kc - 1, :], hT[:, kc - 1, :], mod[:, shift, kc - 1:kc], None,
                                          ALU.add).then_inc(h_made, 1)

            sums_of(PH_SHIFT, acc_even)
            dve.wait_ge(small_in, 16 * N_SMALL)
            for n in range(2):
                link(dve.tensor_tensor(lam_in[:, 2 * n, :], lam_in[:, 2 * n, :], lam_in[:, 2 * n + 1, :], ALU.mult))
                dve.tensor_reduce(lam_sum[:, n:n + 1], lam_in[:, 2 * n, :], AXX, ALU.add).then_inc(lam_dots, 1)
            link(dve.tensor_scalar(gsub[:, :], gsub[:, :], 1.0 - LAMBDA_INIT, None, ALU.mult))
            dve.wait_ge(ss_ready, 1)
            inverse_variance(ps[:, 7, 0:T], D, rs, var_ready)
            dve.wait_ge(lam_e, 1)
            link(dve.tensor_tensor(neg_lam, lam_exp[:, 1:2], lam_exp[:, 0:1], ALU.subtract))
            link(dve.tensor_scalar(neg_lam, neg_lam, -LAMBDA_INIT, None, ALU.add))
            sums_of(PH_SCALE, acc_odd)
            mod_add(0, 2, mod_sum, 2)
            scaled(1, 0)
            dve.wait_ge(mod_ready, 1)
            dve.wait_ge(rs_ready, 1)
            modulated(1, 0, 0)

            def mixed(ph, i, acc, skip=0):
                for j, kind in enumerate(ph.pattern[skip:], skip):
                    if kind == "w":
                        lo(ph, j, i)
                    if kind == "a":
                        ada_step(ph, j, i, acc)

            def glu(first, i):
                dve.wait_ge(gemm_evac, at(i, 2, 2 * first + 2))
                pair = [proj[:, bass.ds(at(i, 2, 2 * first + k), 1), :].rearrange("p o t -> p (o t)")
                        for k in range(2)]
                dst = upad[:, bass.ds(at(i, 1, first), 1), PAD:PAD + T].rearrange("p o t -> p (o t)")
                dve.tensor_tensor(dst, pair[0], pair[1], ALU.mult).then_inc(glu_ready, 1)

            def conv_tap(ch, j, ntap):
                if isinstance(j, int) and j == 0:
                    dve.tensor_scalar(chan(convT, ch), chan(upad, ch)[:, 0:T], wcol(ch, 0), bcol(ch), ALU.mult,
                                      ALU.add).then_inc(tap, 1)
                    return
                dve.wait_ge(tap, ntap)
                dve.scalar_tensor_tensor(chan(convT, ch), chan(upad, ch)[:, bass.ds(j, T)], wcol(ch, j),
                                         chan(convT, ch), ALU.mult, ALU.add).then_inc(tap, 1)

            def chan(buf, ch):
                if isinstance(ch, int):
                    return buf[:, ch, :]
                return buf[:, bass.ds(ch, 1), :].rearrange("p o t -> p (o t)")

            def wcol(ch, j):
                if isinstance(ch, int):
                    return conv_wt[:, ch, bass.ds(j, 1)]
                return conv_wt[:, bass.ds(ch, 1), j:j + 1].rearrange("p o t -> p (o t)")

            def bcol(ch):
                return conv_v[:, 0, ch:ch + 1] if isinstance(ch, int) else conv_v[:, 0, bass.ds(ch, 1)]

            mixed(PH_GLU, None, acc_even)
            with dve.Fori(1, PH_GLU.n) as i:
                mixed(PH_GLU, i, acc_even)
                glu(-1, i)
            mixed(PH_CONV, None, acc_even)
            glu(PH_GLU.n - 1, None)
            dve.wait_ge(glu_ready, 1)
            conv_tap(0, 0, 0)
            with dve.Fori(1, PH_CONV.n) as i:
                mixed(PH_CONV, i, acc_even)
                glu(PH_GLU.n - 1, i)
                for k in range(10):
                    conv_tap(0, i * 10 + (k - 9), i * 10 + (k - 9))

            def qkv(i):
                if i is None:
                    steps = [(1, k, TAPS + k) for k in range(TAPS)]
                else:
                    steps = [(i * 2 + n, k, i * (2 * TAPS) + (2 * k + n - 1)) for k in range(TAPS) for n in range(2)]
                for j, kind in enumerate(PH_QKV.pattern):
                    if kind == "w":
                        lo(PH_QKV, j, i)
                    if kind == "a":
                        ada_step(PH_QKV, j, i, acc_odd)
                    for step in steps[j * len(steps) // PH_QKV.per:(j + 1) * len(steps) // PH_QKV.per]:
                        conv_tap(*step)

            qkv(None)
            glu(CONV_CHUNKS - 1, None)
            dve.wait_ge(glu_ready, CONV_CHUNKS)
            with dve.Fori(1, PH_QKV.n) as i:
                qkv(i)

            def head_scores(h):
                dve.wait_ge(s_ready, h + 1)
                if h >= 2:
                    dve.wait_ge(aT_ready, h - 1)
                for m in range(2):
                    done = dve.scalar_tensor_tensor(probs[:, h % 2, m, :], distm, -SLOPES[h] / SCALE,
                                                    ps[:, 2 + 2 * (h % 2) + m, 0:384], ALU.mult, ALU.add)
                    done.then_inc(s_read_m[m], 1)
                for m in range(2):
                    dve.wait_ge(s_read_m[m], h + 1)
                    for qb, (a, b) in enumerate(((0, 128), (128, 384))):
                        done = dve.tensor_reduce(mx[h % 2][:, 2 * m + qb:2 * m + qb + 1], probs[:, h % 2, m, a:b],
                                                 AXX, ALU.max)
                link(done)
                dve.tensor_scalar(mx[h % 2], mx[h % 2], -SCALE, None, ALU.mult).then_inc(neg_max, 1)

            s_read_m = (s_first, s_read)

            def head_combine(h):
                p, r = probs[:, h % 2], rcp[h % 2]
                dve.wait_ge(exp_done, h + 1)
                link(dve.reciprocal(r, sums[h % 2]))
                link(dve.tensor_scalar(r[:, 2:4], r[:, 2:4], neg_lam, None, ALU.mult))
                for qb, (a, b) in enumerate(((0, 128), (128, 384))):
                    done = dve.tensor_scalar(p[:, 1, a:b], p[:, 1, a:b], r[:, 2 + qb:3 + qb], None, ALU.mult)
                link(done)
                for qb, (a, b) in enumerate(((0, 128), (128, 384))):
                    done = dve.scalar_tensor_tensor(p[:, 0, a:b], p[:, 0, a:b], r[:, qb:qb + 1], p[:, 1, a:b],
                                                    ALU.mult, ALU.add)
                done.then_inc(a_ready, 1)

            head_scores(0)
            head_scores(1)
            for n in range(4):
                dve.wait_ge(vt_ready, n + 1)
                dve.tensor_copy(v_tok[:, 4 * n:4 * n + 4, :],
                                ps[:, 7 * (n % 2), :].rearrange("p (a b) -> p a b", a=4)).then_inc(vt_copied, 1)
            for h in range(HEADS):
                head_combine(h)
                if h == 6:
                    dve.wait_ge(conv_rs, 1)
                    dve.tensor_tensor(convT, convT, bcast_t(stat[:, 1, :], 8), ALU.mult).then_inc(conv_n, 1)
                if h + 2 < HEADS:
                    head_scores(h + 2)
                if h == 3:
                    mod_add(2, 3, mod_sum, 3)
                    dve.tensor_tensor(mod[:, 2, :], mod[:, 2, :], gv[:, 1, :], ALU.mult).then_inc(mod_ready, 1)
                if h == 1:
                    dve.wait_ge(ss_ready, 2)
                    link(dve.tensor_scalar(stat[:, 0, :], ps[:, 7, 0:T], 1.0 / (P * CONV_CHUNKS), None, ALU.mult))
                    dve.tensor_tensor(convT, convT, bcast_t(stat[:, 0, :], 8), ALU.subtract).then_inc(conv_stat, 1)
                if h == 4:
                    dve.wait_ge(ss_ready, 3)
                    inverse_variance(ps[:, 7, 0:T], P * CONV_CHUNKS, stat[:, 1, :], conv_var)
            dve.wait_ge(o_ss, 1)
            inverse_variance(ps[0:HEADS, 7, 0:T], P, o_rs[0:HEADS, :], o_var)

            def low_of(n, src):
                dve.wait_ge(h_hi, KC + n + 1)
                dve.tensor_tensor(a_lo[:, 2 * n:2 * n + 2, :], src, a_hi[:, 2 * n:2 * n + 2, :].bitcast(F32),
                                  ALU.subtract).then_inc(h_ready, 1)

            for n in range(4):
                low_of(n, convT[:, 2 * n:2 * n + 2, :])
            for j in range(2):
                lo(PH_OUT, j, None)
            for n in range(4):
                dve.wait_ge(o_spread, n + 1)
                two = oT[:, 2 * n:2 * n + 2, :].rearrange("p a b -> p (a b)")
                dve.scalar_tensor_tensor(two, two, gsub[:, 0:1], ps[:, 2 + n, :], ALU.mult, ALU.mult)\
                    .then_inc(y_ready, 1)
            for n in range(4):
                dve.wait_ge(y_ready, n + 1)
                low_of(4 + n, oT[:, 2 * n:2 * n + 2, :])

            mixed(PH_OUT, None, acc_even, skip=2)
            with dve.Fori(1, PH_OUT.n) as i:
                mixed(PH_OUT, i, acc_even)

            mod_add(3, 5, mod_sum, 5)
            scaled(4, 2)
            dve.wait_ge(ss_ready, 4)
            inverse_variance(ps[:, 7, 0:T], D, rs, var_ready)
            dve.wait_ge(rs_ready, 2)
            dve.wait_ge(gemm_evac, PH_WQ.block)
            residual(xT, x2_ready)
            for j in range(2):
                lo(PH_WQ, j, None)
            dve.wait_ge(ss_ready, 5)
            inverse_variance(ps[:, 7, 0:T], D, rs, var_ready)
            dve.wait_ge(rs_ready, 3)
            dve.wait_ge(mod_ready, 3)
            dve.wait_ge(x2_ready, 3)
            dve.wait_ge(x2_pool, 1)
            modulated(4, 3, KC)
            for j in range(2, PH_WQ.per):
                lo(PH_WQ, j, None)
            with dve.Fori(1, PH_WQ.n) as i:
                for j in range(PH_WQ.per):
                    lo(PH_WQ, j, i)

            base = count[0]
            with dve.Fori(0, 2 * PEER_HEADS) as r:
                step = [0]

                def chain(ins, before_max=False):
                    step[0] += 1
                    ins.then_inc(vec, 1)
                    dve.wait_ge(vec, r * CHAIN_STEPS + (base + step[0]))
                    if before_max:
                        dve.memset(tiny[:, 7:8], 0.0)

                dve.wait_ge(sc_copied, 8)
                chain(dve.tensor_copy(st.rearrange("p a b -> p (a b)"),
                                      s_all[:, bass.ds(r, 1), :].rearrange("p o n -> p (o n)")), True)
                for half in range(2):
                    d = dve.max(v16[:, half, 0:8], st[:, half, :])
                chain(d, True)
                for half in range(2):
                    dve.max_index(ix16[:, half, 0:8], v16[:, half, 0:8], st[:, half, :])
                    d = dve.match_replace(st2[:, half, :], v16[:, half, 0:8], st[:, half, :], LOWEST)
                chain(d, True)
                for half in range(2):
                    d = dve.max(v16[:, half, 8:16], st2[:, half, :])
                chain(d, True)
                for half in range(2):
                    dve.max_index(ix16[:, half, 8:16], v16[:, half, 8:16], st2[:, half, :])
                chain(dve.tensor_tensor(cand, v16[:, 0, :].unsqueeze(2).to_broadcast([P, TOPK, TOPK]),
                                        v16[:, 1, None, :].to_broadcast([P, TOPK, TOPK]), ALU.add), True)
                flat = cand.rearrange("p a b -> p (a b)")
                chain(dve.max(top16[:, 0:8], flat), True)
                dve.max_index(pos16[:, 0, 0:8], top16[:, 0:8], flat)
                chain(dve.match_replace(cand2, top16[:, 0:8], flat, LOWEST), True)
                chain(dve.max(top16[:, 8:16], cand2), True)
                chain(dve.max_index(pos16[:, 0, 8:16], top16[:, 8:16], cand2))
                dve.tensor_scalar(pos16[:, 1, :], pos16[:, 0, :], 4, None, ALU.logical_shift_right)
                dve.tensor_copy(ix16f, ix16[:, :, :])
                dve.tensor_scalar(gates[:, bass.ds(r, 1), :].rearrange("p o n -> p (o n)"), top16, top16[:, 0:1],
                                  None, ALU.subtract)
                chain(dve.tensor_scalar(pos16[:, 2, :], pos16[:, 0, :], 15, None, ALU.bitwise_and))
                chain(dve.tensor_copy(pos_f, pos16[:, 1:3, :]))
                cols = iota[:, None, 0:TOPK].to_broadcast([P, TOPK, TOPK])
                for which, pick in enumerate((pick_a, pick_b)):
                    d = dve.tensor_tensor(pick, pos_f[:, which, :].unsqueeze(2).to_broadcast([P, TOPK, TOPK]),
                                          cols, ALU.is_equal)
                chain(d)
                for which, pick in enumerate((pick_a, pick_b)):
                    d = dve.tensor_tensor(pick, pick, ix16f[:, which, None, :].to_broadcast([P, TOPK, TOPK]),
                                          ALU.mult)
                chain(d)
                for pick, dst in ((pick_a, idx1), (pick_b, idx2)):
                    d = dve.tensor_reduce(dst[:, bass.ds(r, 1), :].rearrange("p o n -> p (o n)"), pick, AXX,
                                          ALU.add)
                chain(d)
                assert step[0] == CHAIN_STEPS
            count[0] = base + 2 * PEER_HEADS * CHAIN_STEPS
            dve.wait_ge(vec, count[0])
            dve.memset(tiny[:, 6:7], 0.0).then_inc(gate_in, 1)
            dve.wait_ge(gate_exp, 1)
            link(dve.tensor_reduce(gate_sum, gates, AXX, ALU.add))
            link(dve.reciprocal(gate_sum, gate_sum))
            dve.tensor_tensor(gates, gates, gate_sum.unsqueeze(2).to_broadcast([P, 16, TOPK]), ALU.mult)\
                .then_inc(sel_ready, 1)
            dve.wait_ge(selT_ready, 1)
            link(dve.tensor_copy(sel_T[:, 0:2, :], ps[:, 2, :].rearrange("p (a b) -> p a b", a=2)))
            dve.tensor_copy(sel_T[:, 2, :], ps[:, 3, 0:T]).then_inc(selT_copied, 1)
            dve.wait_ge(selT_copied, 1)

            def one_hots(i, j):
                if i is not None:
                    dve.wait_ge(oh_used, at(i, 4, j - 3))
                for which, rows in enumerate((oh1, oh2)):
                    d = dve.tensor_tensor(rows[j], iota[:, None, :].to_broadcast([P, 4, P]),
                                          sel_T[:, which, bass.ds(at(i, 16, 4 * j), 4)].unsqueeze(2)
                                          .to_broadcast([P, 4, P]), ALU.is_equal)
                d.then_inc(oh_ready, 1)

            dve.wait_ge(gemm_evac, PH_GATE.block)
            for j in range(4):
                one_hots(None, j)
            with dve.Fori(1, T // 16) as i:
                for j in range(4):
                    one_hots(i, j)

            def route(b0, i, per):
                dve.wait_ge(gemm_evac, at(i, per, b0 + 1))
                b = b0 - B_UP
                dst = routed_v[:, b, :] if i is None else \
                    routed_v[:, bass.ds(i * per + b, 1), :].rearrange("p o t -> p (o t)")
                dve.tensor_tensor(dst, dst, gel[:, b0 % 2, :], ALU.mult).then_inc(routed, 1)

            def up_body(ph, i, first=False, skip=0):
                for j, kind in enumerate(ph.pattern[skip:], skip):
                    if kind == "a":
                        ada_step(ph, j, i, acc_last)
                    if kind == "w":
                        lo(ph, j, i)
                        if ph.nth(j) % 2 and not (first and ph.nth(j) == 1):
                            route(ph.block + ph.nth(j) // 2 - 1, i, ph.s_per // 2)

            for j in range(2):
                lo(PH_GATE, j, None)
            dve.wait_ge(oh_used, T // 4)
            up_body(PH_GATE, None, True, skip=2)
            with dve.Fori(1, PH_GATE.n) as i:
                up_body(PH_GATE, i)
            with dve.Fori(0, PH_UP.n) as i:
                up_body(PH_UP, i)
            mod_add(5, 6, mod_sum, 6)
            dve.tensor_tensor(mod[:, 5, :], mod[:, 5, :], gv[:, 3, :], ALU.mult).then_inc(mod_ready, 1)
            route(B_END - 1, None, 1)

            def down(i):
                for j in range(PH_DOWN.per):
                    if j % 2 == 0:
                        src = routed_v[:, j // 2, :] if i is None else \
                            routed_v[:, bass.ds(i * (PH_DOWN.per // 2) + j // 2, 1), :].rearrange("p o t -> p (o t)")
                        dve.wait_ge(at_hi, at(i, PH_DOWN.per // 2, j // 2 + 1))
                        dve.tensor_tensor(a_lo[:, j // 2, :], src, a_hi[:, j // 2, :].bitcast(F32), ALU.subtract)\
                            .then_inc(at_lo, 1)
                    lo(PH_DOWN, j, i)

            down(None)
            with dve.Fori(1, PH_DOWN.n) as i:
                down(i)
            for n in range(8):
                dve.wait_ge(split_used, PH_DOWN.s_end - (n < 4))
                for kc in (2 * n, 2 * n + 1):
                    d = dve.tensor_scalar(mixT[:, kc, :], ps[:, n, (kc % 2) * T:(kc % 2 + 1) * T],
                                          mod[:, 5, kc:kc + 1], None, ALU.mult)
                d.then_inc(ff_copied, 1)
            dve.wait_ge(ss_ready, 6)
            inverse_variance(ps[:, 0, 0:T], D, rs, var_ready)
            dve.wait_ge(rs_ready, 4)
            dve.wait_ge(x2_back, 16)
            residual(mixT, out_ready)



CHAIN_STEPS = 14


def kernel(x, c, w_ada, b_ada, g_pre_mix, g_post_mix, g_pre_ffn, g_post_ffn, w_in, lambda_q1, lambda_k1,
           lambda_q2, lambda_k2, g_subln, conv_w, conv_b, conv_ln_g, conv_ln_b, w_out, peer_wq, peer_k1,
           peer_k2, peer_u, peer_v):
    import numpy as np
    import concourse.bacc as bacc
    from concourse.bass_utils import run_bass_kernel_spmd

    def columns(v):
        return np.asarray(v).reshape(-1, P).T

    def blocks(w):
        w = np.asarray(w)
        return np.ascontiguousarray(w.reshape(KC, P, -1, P).transpose(2, 1, 0, 3)).reshape(-1, P, D)

    w_in_b = blocks(w_in[0])
    pairs = np.stack([w_in_b[24:32], w_in_b[32:40]], axis=1).reshape(BLOCKS, P, D)
    w_in_b = np.concatenate([pairs, w_in_b[0:24]])
    u = np.asarray(peer_u[0]).reshape(KEYS, KEYS, KC, P).transpose(0, 3, 2, 1)
    arrays = {
        "x": np.ascontiguousarray(np.asarray(x)[0].T.reshape(KC, P, T).transpose(1, 0, 2)).reshape(P, KC * T),
        "c": np.ascontiguousarray(columns(c)),
        "w_ada": np.asarray(w_ada)[0],
        "b_ada": np.ascontiguousarray(columns(b_ada)),
        "g_vecs": np.ascontiguousarray(np.stack([columns(g) for g in (g_pre_mix, g_post_mix, g_pre_ffn,
                                                                      g_post_ffn)], axis=1)),
        "w_in": w_in_b,
        "lambdas": np.stack([np.asarray(v)[0] for v in (lambda_q1, lambda_k1, lambda_q2, lambda_k2)]),
        "g_subln": np.ascontiguousarray(columns(g_subln)),
        "conv_w": np.ascontiguousarray(np.asarray(conv_w)[0].T.reshape(CONV_CHUNKS, P, TAPS).transpose(1, 0, 2)),
        "conv_vecs": np.ascontiguousarray(np.stack([columns(v) for v in (conv_b, conv_ln_g, conv_ln_b)], axis=1)),
        "w_out": blocks(np.concatenate([np.asarray(w_out)[0, D // 2:], np.asarray(w_out)[0, :D // 2]])),
        "peer_wq": blocks(peer_wq[0]),
        "peer_keys": np.stack([np.asarray(k)[0].T for k in (peer_k1, peer_k2)]),
        "peer_u": np.ascontiguousarray(u).reshape(KEYS, P, D),
        "peer_v": np.asarray(peer_v)[0].reshape(KEYS, P, D),
    }
    nc = bacc.Bacc("TRN2", target_bir_lowering=False, num_devices=1)
    aps = {n: nc.dram_tensor("in_" + n, a.shape, mybir.dt.from_np(a.dtype), kind="ExternalInput").ap()
           for n, a in arrays.items()}
    out = nc.dram_tensor("out_0", (P, KC * T), F32, kind="ExternalOutput").ap()
    build_block(nc, out=out, **aps)
    got = run_bass_kernel_spmd(nc, [{"in_" + n: a for n, a in arrays.items()}], core_ids=[0])
    y = got.results[0]["out_0"].reshape(P, KC, T).transpose(2, 1, 0).reshape(1, T, D)
    return np.ascontiguousarray(y)
```
